# Optimizing a Trainium2 kernel written in Bass

```python
import math
import jax, jax.numpy as jnp
from jax import lax
import numpy as np
import jax
import jax.numpy as jnp

D_MODEL = 1024
BATCH = 1
SEQ = 512
DEPTH = 2

D_MIX = D_MODEL
W_CONV = D_MIX // 4
W_GLA = D_MIX // 4
W_MLA = D_MIX // 4
W_CFM = D_MIX // 4
SC_WIDTH = 3
GLA_HEADS = 4
GLA_DV = W_GLA // GLA_HEADS
GLA_DK = GLA_DV // 2
GLA_LOWRANK = 16
GLA_TAU = 16.0
GLA_CHUNK = 64
MLA_HEADS = 4
MLA_V_DIM = W_MLA // MLA_HEADS
MLA_NOPE = 64
MLA_ROPE = 32
MLA_Q_RANK = 256
MLA_KV_RANK = 128
ROPE_BASE = 10000.0
Q_BLOCK = 128
CFM_WIDTH = 31
D_FF = 2816
FFN_CONV_WIDTH = 3
DN_ALPHA = (2.0 * DEPTH) ** 0.25
DN_BETA = (8.0 * DEPTH) ** -0.25
EPS = 1e-5

SPLIT_SIZES = (
    W_CONV, W_CONV, W_CONV,
    GLA_HEADS * GLA_DK, GLA_HEADS * GLA_DK, W_GLA, W_GLA,
    GLA_LOWRANK, GLA_LOWRANK,
    MLA_Q_RANK, MLA_KV_RANK, MLA_ROPE,
    2 * W_CFM,
)
D_IN = sum(SPLIT_SIZES)


def _split_points():
    pts, acc = [], 0
    for s in SPLIT_SIZES[:-1]:
        acc += s
        pts.append(acc)
    return pts

def layer_norm(x, g, b):
    xf = x.astype(jnp.float32)
    mu = jnp.mean(xf, axis=-1, keepdims=True)
    var = jnp.mean(jnp.square(xf - mu), axis=-1, keepdims=True)
    return ((xf - mu) * lax.rsqrt(var + EPS) * g.astype(jnp.float32) + b.astype(jnp.float32)).astype(x.dtype)

def rms_norm(x, g):
    xf = x.astype(jnp.float32)
    return (xf * lax.rsqrt(jnp.mean(xf * xf, axis=-1, keepdims=True) + EPS) * g.astype(jnp.float32)).astype(x.dtype)

def depthwise_conv(x, w):
    k, c = w.shape
    return lax.conv_general_dilated(
        x, w[:, None, :].astype(x.dtype), window_strides=(1,), padding=[(k // 2, k // 2)],
        dimension_numbers=('NWC', 'WIO', 'NWC'), feature_group_count=c)

def rope_tables(positions):
    inv = ROPE_BASE ** (-jnp.arange(0, MLA_ROPE, 2, dtype=jnp.float32) / MLA_ROPE)
    ang = positions.astype(jnp.float32)[..., None] * inv
    return jnp.cos(ang), jnp.sin(ang)

def apply_rope(x, cos, sin):
    half = MLA_ROPE // 2
    xf = x.astype(jnp.float32)
    x1, x2 = xf[..., :half], xf[..., half:]
    c, s = cos[:, :, None, :], sin[:, :, None, :]
    return jnp.concatenate([x1 * c - x2 * s, x1 * s + x2 * c], axis=-1).astype(x.dtype)

def gla_scan(q, k, v, log_a, include_diag):
    bsz, nh, s, dk = q.shape
    dv = v.shape[-1]
    n = s // GLA_CHUNK

    def chunks(t):
        return t.astype(jnp.float32).reshape(bsz, nh, n, GLA_CHUNK, t.shape[-1]).transpose(2, 0, 1, 3, 4)

    idx = jnp.arange(GLA_CHUNK)
    mask = (idx[:, None] >= idx[None, :]) if include_diag else (idx[:, None] > idx[None, :])
    mask5 = mask[None, None, :, :, None]

    def step(state, inp):
        qc, kc, vc, ac = inp
        b = jnp.cumsum(ac, axis=2)
        o_inter = jnp.einsum('bhtk,bhkv->bhtv', qc * jnp.exp(b), state)
        rel = b[:, :, :, None, :] - b[:, :, None, :, :]
        decay = jnp.where(mask5, jnp.exp(jnp.where(mask5, rel, 0.0)), 0.0)
        scores = jnp.einsum('bhtk,bhsk,bhtsk->bhts', qc, kc, decay)
        o = o_inter + jnp.einsum('bhts,bhsv->bhtv', scores, vc)
        b_last = b[:, :, -1:, :]
        state = jnp.exp(b_last[:, :, 0, :])[..., None] * state + \
            jnp.einsum('bhsk,bhsv->bhkv', kc * jnp.exp(b_last - b), vc)
        return state, o

    init = jnp.zeros((bsz, nh, dk, dv), jnp.float32)
    _, o = lax.scan(step, init, (chunks(q), chunks(k), chunks(v), chunks(log_a)))
    return o.transpose(1, 2, 0, 3, 4).reshape(bsz, nh, s, dv)

def blocked_attention(q, k, v, scale):
    bsz, s, nh, d = q.shape
    nb = s // Q_BLOCK
    qb = q.reshape(bsz, nb, Q_BLOCK, nh, d).transpose(1, 0, 2, 3, 4)

    def blk(qi):
        sc = jnp.einsum('bqhd,bkhd->bhqk', qi, k).astype(jnp.float32) * scale
        p = jax.nn.softmax(sc, axis=-1)
        return jnp.einsum('bhqk,bkhd->bqhd', p.astype(v.dtype), v)

    o = lax.map(blk, qb)
    return o.transpose(1, 0, 2, 3, 4).reshape(bsz, s, nh, v.shape[-1])

def token_mixers(h, cos, sin, w_in, w_sc_conv, w_gla_a_up, b_gla_a, g_gla_head, g_mla_q, w_mla_uq,
                 g_mla_kv, w_mla_ukv, w_cfm_dw, g_cfm_ln, b_cfm_ln, g_branch, w_out):
    bsz, s, _ = h.shape
    proj = h @ w_in
    (sc_b, sc_c, sc_h, gq, gk, gv, gg, ga_f, ga_b, cq, ckv, kr, cfm_in) = jnp.split(proj, _split_points(), axis=-1)

    y_a = sc_b * depthwise_conv(sc_c * sc_h, w_sc_conv)

    def heads(t, d):
        return t.reshape(bsz, s, GLA_HEADS, d).transpose(0, 2, 1, 3)

    q = heads(gq, GLA_DK) * (GLA_DK ** -0.5)
    k = heads(gk, GLA_DK)
    v = heads(gv, GLA_DV)
    la_f = heads(jax.nn.log_sigmoid((ga_f @ w_gla_a_up[0] + b_gla_a[0]).astype(jnp.float32)) / GLA_TAU, GLA_DK)
    la_b = heads(jax.nn.log_sigmoid((ga_b @ w_gla_a_up[1] + b_gla_a[1]).astype(jnp.float32)) / GLA_TAU, GLA_DK)
    flip = lambda t: jnp.flip(t, axis=2)
    o_f = gla_scan(q, k, v, la_f, True)
    o_b = flip(gla_scan(flip(q), flip(k), flip(v), flip(la_b), False))
    o = (o_f + o_b).transpose(0, 2, 1, 3)
    o = rms_norm(o, g_gla_head.reshape(GLA_HEADS, GLA_DV)).reshape(bsz, s, W_GLA)
    y_b = o.astype(h.dtype) * jax.nn.silu(gg)

    qm = (rms_norm(cq, g_mla_q) @ w_mla_uq).reshape(bsz, s, MLA_HEADS, MLA_NOPE + MLA_ROPE)
    q_c = jnp.concatenate([qm[..., :MLA_NOPE], apply_rope(qm[..., MLA_NOPE:], cos, sin)], axis=-1)
    kvm = (rms_norm(ckv, g_mla_kv) @ w_mla_ukv).reshape(bsz, s, MLA_HEADS, MLA_NOPE + MLA_V_DIM)
    k_rope = jnp.broadcast_to(apply_rope(kr[:, :, None, :], cos, sin), (bsz, s, MLA_HEADS, MLA_ROPE))
    k_c = jnp.concatenate([kvm[..., :MLA_NOPE], k_rope], axis=-1)
    v_c = kvm[..., MLA_NOPE:]
    y_c = blocked_attention(q_c, k_c, v_c, (MLA_NOPE + MLA_ROPE) ** -0.5).reshape(bsz, s, W_MLA)

    a, gate = jnp.split(cfm_in, 2, axis=-1)
    u = depthwise_conv(a * jax.nn.sigmoid(gate), w_cfm_dw)
    y_d = jax.nn.silu(layer_norm(u, g_cfm_ln, b_cfm_ln))

    gains = jnp.split(g_branch, [W_CONV, W_CONV + W_GLA, W_CONV + W_GLA + W_MLA])
    y = jnp.concatenate([rms_norm(yb, gb) for yb, gb in zip((y_a, y_b, y_c, y_d), gains)], axis=-1)
    return y @ w_out

def conv_ffn(h, w_up, w_dw, w_down):
    u = depthwise_conv(h @ w_up, w_dw)
    g, val = jnp.split(u, 2, axis=-1)
    return (jax.nn.silu(g) * val) @ w_down

def first_inputs(seed: int = 0) -> dict:
    key = jax.random.key(seed)
    ks = jax.random.split(key, 32)
    L = DEPTH
    nrm = lambda k, shape, scale: jax.random.normal(k, shape, jnp.float32) * scale
    gain = lambda k, shape: 1.0 + 0.02 * jax.random.normal(k, shape, jnp.float32)
    offsets = jax.random.randint(ks[1], (BATCH, 1), 0, SEQ, dtype=jnp.int32)
    positions = jnp.arange(SEQ, dtype=jnp.int32)[None, :] + offsets
    return {
        'x': jax.random.normal(ks[0], (BATCH, SEQ, D_MODEL), jnp.float32),
        'positions': positions,
        'ln_in_g': gain(ks[2], (D_MODEL,)),
        'ln_in_b': nrm(ks[3], (D_MODEL,), 0.02),
        'w_in': nrm(ks[4], (L, D_MODEL, D_IN), D_MODEL ** -0.5),
        'w_sc_conv': nrm(ks[5], (L, SC_WIDTH, W_CONV), SC_WIDTH ** -0.5),
        'w_gla_a_up': nrm(ks[6], (L, 2, GLA_LOWRANK, GLA_HEADS * GLA_DK), GLA_LOWRANK ** -0.5),
        'b_gla_a': nrm(ks[7], (L, 2, GLA_HEADS * GLA_DK), 0.02),
        'g_gla_head': gain(ks[8], (L, W_GLA)),
        'g_mla_q': gain(ks[9], (L, MLA_Q_RANK)),
        'w_mla_uq': nrm(ks[10], (L, MLA_Q_RANK, MLA_HEADS * (MLA_NOPE + MLA_ROPE)), MLA_Q_RANK ** -0.5),
        'g_mla_kv': gain(ks[11], (L, MLA_KV_RANK)),
        'w_mla_ukv': nrm(ks[12], (L, MLA_KV_RANK, MLA_HEADS * (MLA_NOPE + MLA_V_DIM)), MLA_KV_RANK ** -0.5),
        'w_cfm_dw': nrm(ks[13], (L, CFM_WIDTH, W_CFM), CFM_WIDTH ** -0.5),
        'g_cfm_ln': gain(ks[14], (L, W_CFM)),
        'b_cfm_ln': nrm(ks[15], (L, W_CFM), 0.02),
        'g_branch': gain(ks[16], (L, D_MIX)),
        'w_out': nrm(ks[17], (L, D_MIX, D_MODEL), DN_BETA * D_MIX ** -0.5),
        'ln1_g': gain(ks[18], (L, D_MODEL)),
        'ln1_b': nrm(ks[19], (L, D_MODEL), 0.02),
        'w_ffn_up': nrm(ks[20], (L, D_MODEL, 2 * D_FF), D_MODEL ** -0.5),
        'w_ffn_dw': nrm(ks[21], (L, FFN_CONV_WIDTH, 2 * D_FF), FFN_CONV_WIDTH ** -0.5),
        'w_ffn_down': nrm(ks[22], (L, D_FF, D_MODEL), DN_BETA * D_FF ** -0.5),
        'ln2_g': gain(ks[23], (L, D_MODEL)),
        'ln2_b': nrm(ks[24], (L, D_MODEL), 0.02),
    }

def first_block(x, positions, ln_in_g, ln_in_b, w_in, w_sc_conv, w_gla_a_up, b_gla_a, g_gla_head, g_mla_q,
              w_mla_uq, g_mla_kv, w_mla_ukv, w_cfm_dw, g_cfm_ln, b_cfm_ln, g_branch, w_out, ln1_g, ln1_b,
              w_ffn_up, w_ffn_dw, w_ffn_down, ln2_g, ln2_b):
    cos, sin = rope_tables(positions)
    h = layer_norm(x, ln_in_g, ln_in_b)
    for l in range(DEPTH):
        mix = token_mixers(h, cos, sin, w_in[l], w_sc_conv[l], w_gla_a_up[l], b_gla_a[l], g_gla_head[l],
                           g_mla_q[l], w_mla_uq[l], g_mla_kv[l], w_mla_ukv[l], w_cfm_dw[l], g_cfm_ln[l],
                           b_cfm_ln[l], g_branch[l], w_out[l])
        h = layer_norm(DN_ALPHA * h + mix, ln1_g[l], ln1_b[l])
        h = layer_norm(DN_ALPHA * h + conv_ffn(h, w_ffn_up[l], w_ffn_dw[l], w_ffn_down[l]), ln2_g[l], ln2_b[l])
    return h


DEPTH_2 = 1

CTX_LEN = 256
GRID_W = 64

MIX_W = 2 * D_MODEL
SSD_HEADDIM = 64
SSD_W = 3 * MIX_W // 4
SSD_HEADS = SSD_W // SSD_HEADDIM
SSD_GROUPS = 4
SSD_HPG = SSD_HEADS // SSD_GROUPS
SSD_STATE = 128
SSD_CONV = 5
SSD_CHUNK = 128
CONV_CH = SSD_W + 2 * SSD_GROUPS * SSD_STATE
XBCDT_COLS = CONV_CH + 2 * SSD_HEADS
POOL_W = MIX_W - SSD_W
POOL_WINDOWS = (2, 4, 8, 16)
POOL_GROUPS = len(POOL_WINDOWS)
POOL_GW = POOL_W // POOL_GROUPS
IN_COLS = XBCDT_COLS + SSD_W + POOL_W
N_EXPERTS = 32
TOP_K = 4
D_FF_2 = D_MODEL
SWIGLU_ALPHA = 1.702
SWIGLU_LIMIT = 7.0
MOE_BLOCK = 128
RMS_EPS = 1e-6


def rmsnorm(h, w):
    hf = h.astype(jnp.float32)
    hf = hf * lax.rsqrt(jnp.mean(hf * hf, axis=-1, keepdims=True) + RMS_EPS)
    return (hf * w.astype(jnp.float32)).astype(h.dtype)

def modulate(h, shift, scale):
    return h * (1 + scale) + shift

def dwconv_centred(u, w, b):
    ch = u.shape[-1]
    y = lax.conv_general_dilated(
        u, w[:, None, :].astype(u.dtype), window_strides=(1,),
        padding=[(SSD_CONV // 2, SSD_CONV // 2)],
        dimension_numbers=("NWC", "WIO", "NWC"), feature_group_count=ch)
    return y + b.astype(u.dtype)

def segsum(a):
    t = a.shape[-1]
    cs = jnp.cumsum(a, axis=-1)
    diff = cs[..., :, None] - cs[..., None, :]
    return jnp.where(np.tril(np.ones((t, t), dtype=bool)), diff, -jnp.inf)

def ssd_direction_inputs(xbc, dt_raw, dt_bias, a_log, d):
    dtr = dt_raw[..., d, :]
    if d == 1:
        xbc = xbc[:, ::-1]
        dtr = dtr[:, ::-1]
    b, L, _ = xbc.shape
    gn = SSD_GROUPS * SSD_STATE
    xh = xbc[..., :SSD_W].reshape(b, L, SSD_GROUPS, SSD_HPG, SSD_HEADDIM).astype(jnp.float32)
    bm = xbc[..., SSD_W:SSD_W + gn].reshape(b, L, SSD_GROUPS, SSD_STATE).astype(jnp.float32)
    cm = xbc[..., SSD_W + gn:].reshape(b, L, SSD_GROUPS, SSD_STATE).astype(jnp.float32)
    dt = jax.nn.softplus(dtr.astype(jnp.float32) + dt_bias[d].astype(jnp.float32))
    dt = dt.reshape(b, L, SSD_GROUPS, SSD_HPG)
    log_a = -jnp.exp(a_log[d].astype(jnp.float32)).reshape(SSD_GROUPS, SSD_HPG) * dt
    return xh * dt[..., None], log_a, bm, cm

def ssd_chunked(xs, log_a, bm, cm, init_state):
    b, L, G, E, P = xs.shape
    n = bm.shape[-1]
    nc = L // SSD_CHUNK
    xs = xs.reshape(b, nc, SSD_CHUNK, G, E, P)
    bm = bm.reshape(b, nc, SSD_CHUNK, G, n)
    cm = cm.reshape(b, nc, SSD_CHUNK, G, n)
    a = jnp.moveaxis(log_a.reshape(b, nc, SSD_CHUNK, G, E), 2, -1)
    a_cs = jnp.cumsum(a, axis=-1)
    lmat = jnp.exp(segsum(a))
    cb = jnp.einsum("bclgn,bcsgn->bcgls", cm, bm)
    y_diag = jnp.einsum("bcgls,bcgels,bcsgep->bclgep", cb, lmat, xs)
    decay_states = jnp.exp(a_cs[..., -1:] - a_cs)
    states = jnp.einsum("bclgn,bcgel,bclgep->bcgepn", bm, decay_states, xs)
    states = jnp.concatenate([init_state[:, None], states], axis=1)
    chunk_end = jnp.pad(a_cs[..., -1], ((0, 0), (1, 0), (0, 0), (0, 0)))
    decay_chunk = jnp.exp(segsum(jnp.moveaxis(chunk_end, 1, -1)))
    new_states = jnp.einsum("bgezy,bygepn->bzgepn", decay_chunk, states)
    prev_states, final_state = new_states[:, :-1], new_states[:, -1]
    y_off = jnp.einsum("bclgn,bcgepn,bcgel->bclgep", cm, prev_states, jnp.exp(a_cs))
    return (y_diag + y_off).reshape(b, L, G, E, P), final_state

def ssd_final_state(xbc, dt_raw, dt_bias, a_log, d):
    xs, log_a, bm, _ = ssd_direction_inputs(xbc, dt_raw, dt_bias, a_log, d)
    a_cs = jnp.cumsum(log_a, axis=1)
    w = jnp.exp(a_cs[:, -1:] - a_cs)
    return jnp.einsum("blgn,blge,blgep->bgepn", bm, w, xs)

def ssd_bidir(xbc, dt_raw, dt_bias, a_log, d_skip, init_states):
    b, L, _ = xbc.shape
    xs_f, la_f, bm_f, cm_f = ssd_direction_inputs(xbc, dt_raw, dt_bias, a_log, 0)
    y_f, fin_f = ssd_chunked(xs_f, la_f, bm_f, cm_f, init_states[0])
    xs_b, la_b, bm_b, cm_b = ssd_direction_inputs(xbc, dt_raw, dt_bias, a_log, 1)
    y_b, fin_b = ssd_chunked(xs_b, la_b, bm_b, cm_b, init_states[1])
    x_heads = xbc[..., :SSD_W].reshape(b, L, SSD_HEADS, SSD_HEADDIM).astype(jnp.float32)
    y = (y_f + y_b[:, ::-1]).reshape(b, L, SSD_W) \
        + (x_heads * d_skip.astype(jnp.float32)[:, None]).reshape(b, L, SSD_W)
    return y.astype(xbc.dtype), fin_f, fin_b

def centred_mean_minus_self(u, window):
    wl = u.shape[1]
    cs = jnp.pad(jnp.cumsum(u.astype(jnp.float32), axis=1), ((0, 0), (1, 0), (0, 0)))
    t = np.arange(wl)
    lo = np.clip(t - window // 2, 0, wl)
    hi = np.clip(t + window - window // 2, 0, wl)
    cnt = (hi - lo).astype(np.float32)
    mean = (cs[:, hi] - cs[:, lo]) / cnt[None, :, None]
    return mean.astype(u.dtype) - u

def pool_mixer(u, pool_w, pool_scale):
    n, wl, _ = u.shape
    ug = u.reshape(n, wl, POOL_GROUPS, POOL_GW)
    pooled = jnp.stack([centred_mean_minus_self(ug[:, :, g], w)
                        for g, w in enumerate(POOL_WINDOWS)], axis=2)
    y = jnp.einsum("nwgi,gio->nwgo", pooled, pool_w)
    return y.reshape(n, wl, POOL_W) * pool_scale

def mixer_out(y_ssd, z, y_pool, ssd_norm_w, w_out):
    y_ssd = rmsnorm(y_ssd * jax.nn.silu(z), ssd_norm_w)
    return jnp.concatenate([y_ssd, y_pool], axis=-1) @ w_out

def moe_ffn(h, router_w, router_b, w1, b1, w2, b2):
    shp = h.shape
    xt = h.reshape(-1, shp[-1])
    t = xt.shape[0]
    logits = (xt @ router_w + router_b).astype(jnp.float32)
    top_val, top_idx = lax.top_k(logits, TOP_K)
    gates = jax.nn.softmax(top_val, axis=-1)
    e_flat = top_idx.reshape(-1).astype(jnp.int32)
    tok_flat = jnp.repeat(jnp.arange(t, dtype=jnp.int32), TOP_K)
    g_flat = gates.reshape(-1)
    n_assign = t * TOP_K
    order = jnp.argsort(e_flat)
    e_sorted = e_flat[order]
    counts = jnp.bincount(e_flat, length=N_EXPERTS).astype(jnp.int32)
    padded = (counts + MOE_BLOCK - 1) // MOE_BLOCK * MOE_BLOCK
    pad_end = jnp.cumsum(padded)
    pad_start = pad_end - padded
    grp_start = jnp.cumsum(counts) - counts
    rank = jnp.arange(n_assign, dtype=jnp.int32) - grp_start[e_sorted]
    dest = pad_start[e_sorted] + rank
    n_blocks = -(-n_assign // MOE_BLOCK) + N_EXPERTS
    n_slots = n_blocks * MOE_BLOCK
    slot_tok = jnp.full((n_slots,), t, jnp.int32).at[dest].set(tok_flat[order])
    slot_gate = jnp.zeros((n_slots,), jnp.float32).at[dest].set(g_flat[order])
    block_start = jnp.arange(n_blocks, dtype=jnp.int32) * MOE_BLOCK
    block_exp = jnp.minimum(jnp.searchsorted(pad_end, block_start, side="right"),
                            N_EXPERTS - 1).astype(jnp.int32)
    x_pad = jnp.concatenate([xt, jnp.zeros((1, shp[-1]), xt.dtype)], axis=0)

    def run_block(args):
        toks, e = args
        hb = x_pad[toks] @ w1[e] + b1[e]
        g_part = jnp.minimum(hb[..., ::2], SWIGLU_LIMIT)
        u_part = jnp.clip(hb[..., 1::2], -SWIGLU_LIMIT, SWIGLU_LIMIT)
        act = g_part * jax.nn.sigmoid(SWIGLU_ALPHA * g_part) * (u_part + 1)
        return act @ w2[e] + b2[e]

    y_slots = lax.map(run_block, (slot_tok.reshape(n_blocks, MOE_BLOCK), block_exp))
    y_slots = y_slots.reshape(n_slots, shp[-1]) * slot_gate[:, None].astype(xt.dtype)
    out = jnp.zeros((t + 1, shp[-1]), xt.dtype).at[slot_tok].add(y_slots)[:t]
    return out.reshape(shp)

def second_inputs(seed: int = 0) -> dict:
    key = jax.random.key(seed)
    ks = jax.random.split(key, 25)
    f32 = jnp.float32

    def nrm(k, shape, s):
        return jax.random.normal(k, shape, f32) * s

    dt0 = jnp.exp(jax.random.uniform(ks[10], (DEPTH_2, 2, SSD_HEADS), f32,
                                     math.log(1e-3), math.log(1e-1)))
    return {
        "x": nrm(ks[0], (BATCH, SEQ, D_MODEL), 1.0),
        "c": nrm(ks[1], (BATCH, D_MODEL), 1.0),
        "ctx": nrm(ks[2], (BATCH, CTX_LEN, D_MODEL), 1.0),
        "c_ctx": nrm(ks[3], (D_MODEL,), 1.0),
        "w_mod": nrm(ks[4], (DEPTH_2, D_MODEL, 6 * D_MODEL), 0.5 * D_MODEL ** -0.5),
        "b_mod": nrm(ks[5], (DEPTH_2, 6 * D_MODEL), 0.01),
        "norm1_w": 1.0 + nrm(ks[6], (DEPTH_2, D_MODEL), 0.02),
        "norm2_w": 1.0 + nrm(ks[7], (DEPTH_2, D_MODEL), 0.02),
        "w_in": nrm(ks[8], (DEPTH_2, D_MODEL, IN_COLS), D_MODEL ** -0.5),
        "conv_w": nrm(ks[9], (DEPTH_2, SSD_CONV, CONV_CH), SSD_CONV ** -0.5),
        "conv_b": nrm(ks[11], (DEPTH_2, CONV_CH), 0.01),
        "dt_bias": dt0 + jnp.log(-jnp.expm1(-dt0)),
        "a_log": jnp.log(jax.random.uniform(ks[12], (DEPTH_2, 2, SSD_HEADS), f32, 1.0, 16.0)),
        "d_skip": 1.0 + nrm(ks[13], (DEPTH_2, SSD_HEADS), 0.1),
        "ssd_norm_w": 1.0 + nrm(ks[14], (DEPTH_2, SSD_W), 0.02),
        "pool_w": nrm(ks[15], (DEPTH_2, POOL_GROUPS, POOL_GW, POOL_GW), POOL_GW ** -0.5),
        "pool_scale": 1.0 + nrm(ks[16], (DEPTH_2, POOL_W), 0.1),
        "w_out": nrm(ks[17], (DEPTH_2, MIX_W, D_MODEL), MIX_W ** -0.5),
        "router_w": nrm(ks[18], (DEPTH_2, D_MODEL, N_EXPERTS), D_MODEL ** -0.5),
        "router_b": nrm(ks[19], (DEPTH_2, N_EXPERTS), 0.01),
        "w1": nrm(ks[20], (DEPTH_2, N_EXPERTS, D_MODEL, 2 * D_FF_2), D_MODEL ** -0.5),
        "b1": nrm(ks[21], (DEPTH_2, N_EXPERTS, 2 * D_FF_2), 0.01),
        "w2": nrm(ks[22], (DEPTH_2, N_EXPERTS, D_FF_2, D_MODEL), D_FF_2 ** -0.5),
        "b2": nrm(ks[23], (DEPTH_2, N_EXPERTS, D_MODEL), 0.01),
        "final_norm_w": 1.0 + nrm(ks[24], (D_MODEL,), 0.02),
    }

def second_block(x, c, ctx, c_ctx, w_mod, b_mod, norm1_w, norm2_w, w_in, conv_w, conv_b,
              dt_bias, a_log, d_skip, ssd_norm_w, pool_w, pool_scale, w_out,
              router_w, router_b, w1, b1, w2, b2, final_norm_w):
    b, L, _ = x.shape
    rows = L // GRID_W
    zero_state = jnp.zeros((b, SSD_GROUPS, SSD_HPG, SSD_HEADDIM, SSD_STATE), jnp.float32)
    for l in range(DEPTH_2):
        last = l == DEPTH_2 - 1
        mod = (jax.nn.silu(c) @ w_mod[l] + b_mod[l])[:, None, :]
        mod_c = jax.nn.silu(c_ctx) @ w_mod[l] + b_mod[l]
        sh1, sc1, g1, sh2, sc2, g2 = jnp.split(mod, 6, axis=-1)
        csh1, csc1, cg1, csh2, csc2, cg2 = jnp.split(mod_c, 6, axis=-1)

        hc = modulate(rmsnorm(ctx, norm1_w[l]), csh1, csc1)
        pc = hc @ w_in[l][:, :(XBCDT_COLS if last else IN_COLS)]
        xbc_c = jax.nn.silu(dwconv_centred(pc[..., :CONV_CH], conv_w[l], conv_b[l]))
        dt_c = pc[..., CONV_CH:XBCDT_COLS].reshape(b, -1, 2, SSD_HEADS)
        if last:
            init_states = (ssd_final_state(xbc_c, dt_c, dt_bias[l], a_log[l], 0),
                           ssd_final_state(xbc_c, dt_c, dt_bias[l], a_log[l], 1))
            ctx_next = ctx
        else:
            y_c, fin_cf, fin_cb = ssd_bidir(xbc_c, dt_c, dt_bias[l], a_log[l], d_skip[l],
                                            (zero_state, zero_state))
            init_states = (fin_cf, fin_cb)
            yp_c = pool_mixer(pc[..., XBCDT_COLS + SSD_W:], pool_w[l], pool_scale[l])
            ctx_next = ctx + cg1 * mixer_out(y_c, pc[..., XBCDT_COLS:XBCDT_COLS + SSD_W],
                                             yp_c, ssd_norm_w[l], w_out[l])
            ctx_next = ctx_next + cg2 * moe_ffn(
                modulate(rmsnorm(ctx_next, norm2_w[l]), csh2, csc2),
                router_w[l], router_b[l], w1[l], b1[l], w2[l], b2[l])

        hx = modulate(rmsnorm(x, norm1_w[l]), sh1, sc1)
        p = hx @ w_in[l]
        xbc = jax.nn.silu(dwconv_centred(p[..., :CONV_CH], conv_w[l], conv_b[l]))
        dt_x = p[..., CONV_CH:XBCDT_COLS].reshape(b, L, 2, SSD_HEADS)
        y_x, _, _ = ssd_bidir(xbc, dt_x, dt_bias[l], a_log[l], d_skip[l], init_states)
        u_pool = p[..., XBCDT_COLS + SSD_W:].reshape(b * rows, GRID_W, POOL_W)
        y_pool = pool_mixer(u_pool, pool_w[l], pool_scale[l]).reshape(b, L, POOL_W)
        x = x + g1 * mixer_out(y_x, p[..., XBCDT_COLS:XBCDT_COLS + SSD_W], y_pool,
                               ssd_norm_w[l], w_out[l])
        x = x + g2 * moe_ffn(modulate(rmsnorm(x, norm2_w[l]), sh2, sc2),
                             router_w[l], router_b[l], w1[l], b1[l], w2[l], b2[l])
        ctx = ctx_next
    return rmsnorm(x, final_norm_w)


def setup_inputs(seed=0):
    out = dict(first_inputs(seed))
    for name, value in second_inputs(seed + 1).items():
        if name != "x":
            out[name + "_2"] = value
    return out


def reference(
    x, positions, ln_in_g, ln_in_b, w_in, w_sc_conv, w_gla_a_up, b_gla_a, g_gla_head, g_mla_q,
    w_mla_uq, g_mla_kv, w_mla_ukv, w_cfm_dw, g_cfm_ln, b_cfm_ln, g_branch, w_out, ln1_g, ln1_b,
    w_ffn_up, w_ffn_dw, w_ffn_down, ln2_g, ln2_b, c_2, ctx_2, c_ctx_2, w_mod_2, b_mod_2,
    norm1_w_2, norm2_w_2, w_in_2, conv_w_2, conv_b_2, dt_bias_2, a_log_2, d_skip_2,
    ssd_norm_w_2, pool_w_2, pool_scale_2, w_out_2, router_w_2, router_b_2, w1_2, b1_2, w2_2,
    b2_2, final_norm_w_2,
):
    x = first_block(
        x, positions, ln_in_g, ln_in_b, w_in, w_sc_conv, w_gla_a_up, b_gla_a, g_gla_head,
        g_mla_q, w_mla_uq, g_mla_kv, w_mla_ukv, w_cfm_dw, g_cfm_ln, b_cfm_ln, g_branch, w_out,
        ln1_g, ln1_b, w_ffn_up, w_ffn_dw, w_ffn_down, ln2_g, ln2_b,
    )
    return second_block(
        x, c_2, ctx_2, c_ctx_2, w_mod_2, b_mod_2, norm1_w_2, norm2_w_2, w_in_2, conv_w_2,
        conv_b_2, dt_bias_2, a_log_2, d_skip_2, ssd_norm_w_2, pool_w_2, pool_scale_2, w_out_2,
        router_w_2, router_b_2, w1_2, b1_2, w2_2, b2_2, final_norm_w_2,
    )


_drawn_inputs = setup_inputs


def setup_inputs(seed=0):
    import zlib

    import numpy as np

    out = dict(_drawn_inputs(seed))
    spreads = {}
    factors = {'b_gla_a': 8.0,
     'g_gla_head': 6.704,
     'g_mla_q': 6.305,
     'g_mla_kv': 4.272,
     'g_cfm_ln': 5.17,
     'b_cfm_ln': 4.92,
     'g_branch': 3.417,
     'ctx_2': 7.158,
     'c_ctx_2': 8.0,
     'b_mod_2': 2.88,
     'norm1_w_2': 5.312,
     'norm2_w_2': 3.384,
     'conv_b_2': 21.996,
     'd_skip_2': 35.232,
     'ssd_norm_w_2': 6.205,
     'pool_scale_2': 2.799,
     'router_b_2': 6.975,
     'b1_2': 24.877,
     'b2_2': 64.0,
     'final_norm_w_2': 8.148}
    for name, (base, spread) in spreads.items():
        noise = np.random.default_rng([zlib.crc32(name.encode()), seed]).standard_normal(out[name].shape)
        drawn = base * np.exp(spread * noise) if base else spread * noise
        out[name] = jnp.asarray(drawn.astype(out[name].dtype))
    for name, factor in factors.items():
        out[name] = (out[name] * factor).astype(out[name].dtype)
    return out
```

```python
from contextlib import ExitStack

import numpy as np

import concourse.bass as bass
from concourse import mybir

P = 128
T = 512
TB = T // P
D = 1024
KD = D // P
DEPTH = 2
D_FF = 2816
KF = D_FF // P
HEADS = 4
DK = 32
DV = 64
NOPE = 64
ROPE = 32
MIX = 256
SUB = 16
NSUB = P // SUB
CFM_TAPS = 31
FFN_TAPS = 3
GLA_TAU = 16.0
GRID_W = 64
GRID_ROWS = T // GRID_W
POOL_WINDOWS = (2, 4, 8, 16)
POOL_PAD = max(POOL_WINDOWS) // 2
CTX = 256
CB = CTX // P
NB = TB + CB
GROUPS = 4
HPG = 6
SSD_HEADS = GROUPS * HPG
HEAD_W = 64
SSD_W = SSD_HEADS * HEAD_W
GW = HPG * HEAD_W
XC = SSD_W // P
SSD_TAPS = 5
DT_W = 2 * SSD_HEADS
EXPERTS = 32
TOP_K = 4
BACK_BANK = [4, 5, 6, 7, 4, 5, 6, 7]
SPLITS = 4
MOE_TILES = 3 * KD
NO_LOGIT = -3e38
PICKED = 3e38
SWIGLU_ALPHA = 1.702
SWIGLU_LIMIT = 7.0
MAX_BLOCKS = T * TOP_K // P + EXPERTS
ALPHA = (2.0 * DEPTH) ** 0.25
EPS = 1e-5
EPS2 = 1e-6
RING = 8
TILE = 1024
TWO_PI = 2.0 * np.pi
WORK = 26016
ROUNDER = float(1.5 * 2 ** 23)

F32 = mybir.dt.float32
F32R = mybir.dt.float32r
I32 = mybir.dt.int32
ALU = mybir.AluOpType
ACT = mybir.ActivationFunctionType
AX = mybir.AxisListType.X

COMMON_COLS = [("ln_in_g", 8), ("ln_in_b", 8)]
LAYER_COLS = [("sc_w", 6), ("gla_b", 2), ("gla_head_g", 2), ("mla_q_g", 2), ("mla_kv_g", 1), ("cfm_w", 62),
              ("cfm_g", 2), ("cfm_b", 2), ("branch_g", 8), ("ln1_g", 8), ("ln1_b", 8),
              ("ffn_w", 3 * 2 * KF), ("ln2_g", 8), ("ln2_b", 8)]
BLOCK2_COLS = [("cond", 16), ("b_mod", 48), ("norm1_w", 8), ("norm2_w", 8), ("final_w", 8),
               ("conv_w", SSD_TAPS * (XC + 2 * GROUPS)), ("conv_b", XC + 2 * GROUPS), ("ssd_norm_w", XC), ("pool_scale", 4)]
ROWS = [("dt_bias", DT_W), ("a_log", DT_W), ("d_skip", SSD_HEADS), ("router_b", EXPERTS)]
CONST_COLS = [("ident", P), ("ones", P), ("ones_d", P), ("ones_mix", P), ("heads64", P), ("upto", P), ("after", P),
              ("inv_freq", 1), ("eps", 1), ("sin_sign", 1), ("eps2", 1), ("before", P), ("from", P), ("pool_share", len(POOL_WINDOWS) * GRID_W)]


def offsets(spec, start=0):
    out, at = {}, start
    for name, n in spec:
        out[name] = (at, n)
        at += n
    return out, at


COMMON_AT, at_ = offsets(COMMON_COLS)
LAYER_AT, LAYER_N = offsets(LAYER_COLS)
BLOCK2_AT, BLOCK2_N = offsets(BLOCK2_COLS, at_ + DEPTH * LAYER_N)
NCOLS = BLOCK2_N
ROW_AT, NROWS = offsets(ROWS)
CONST_AT, NCONST = offsets(CONST_COLS)

PROJ = ["a0", "a1", "gate0", "gate1", "misc", "ckv", "cq0", "cq1", "q", "k",
        "b0", "b1", "c0", "c1", "h0", "h1", "gg0", "gg1"]
SLOT = {n: i for i, n in enumerate(PROJ)}


class Count:

    def __init__(self, key, found, prefix=()):
        self.key, self.found, self.prefix, self.n = key, found, prefix, 0

    def note(self, *name):
        self.found[self.prefix + name] = (self.key, self.n)

    def up(self, *names):
        self.n += 1
        for name in names:
            self.note(*name)
        return 1

    def all_but(self, last):
        return max(self.n - last, 0)

    def close(self):
        self.found[("per_turn", self.key)] = (self.key, self.n)


def build(nc, io, marks, found):
    with ExitStack() as ctx:
        def sb(name, shape, dt=F32):
            return ctx.enter_context(nc.sbuf_tensor("sb_" + name, shape, dt))

        def sem(name):
            return ctx.enter_context(nc.semaphore(name))

        pe_done, act_done, dve_done = sem("pe_done"), sem("act_done"), sem("dve_done")
        moe_pe_done, moe_act_done, moe_dve_done = sem("moe_pe_done"), sem("moe_act_done"), sem("moe_dve_done")
        moe_pool_done = sem("moe_pool_done")
        s_iota = sem("iota_loaded")
        s_bias = sem("expert_biases_loaded")
        s_hi = sem("weight_hi_made")
        s_freed = sem("weight_parts_used")
        sems = {"pe": pe_done, "act": act_done, "dve": dve_done}
        s_in = sem("inputs_loaded")
        s_out = sem("output_stored")
        s_ctx = sem("context_loaded")
        s_used = sem("weight_tile_used")
        s_tile = [sem(f"weight_slot{r}_loaded") for r in range(RING)]
        banks = [ctx.enter_context(nc.psum_tensor(f"bank{i}", [P, 512], F32)) for i in range(8)]

        cols = sb("cols", [P, NCOLS])
        consts = sb("consts", [P, NCONST])
        ring = sb("ring", [P, RING, TILE])
        hT = sb("hT", [P, KD, T])
        x_at = -(-nc.sbuf_base // 32) * 32
        xT = sb("xT", [P, KD, T])
        sq = sb("sq", [P, KD, T])
        rows_sb = sb("rows", [P, NROWS])
        csil = sb("csil", [P, 16])
        modv = sb("modv", [P, 48, 2])
        gains = sb("gains", [P, 3, KD])
        rstd = sb("rstd", [P, 2, T])
        turn_tables = sb("turn_tables", [P, 2, T])
        cos_t, sin_t = turn_tables[:, 0, :], turn_tables[:, 1, :]
        pos_i = sq[:, 0, :].bitcast(I32)
        padc = sb("padc", [P, 2, T + CFM_TAPS - 1])
        pads = sb("pads", [P, 2, T + 2])
        work_at = -(-nc.sbuf_base // 32) * 32
        work = sb("work", [P, WORK])

        def const(name):
            a, n = CONST_AT[name]
            return consts[:, a:a + n]

        def col(l, name, i=0):
            a = COMMON_AT[name][0] if l is None else at_ + l * LAYER_N + LAYER_AT[name][0]
            return cols[:, a + i:a + i + 1]

        def col2(name, i=0, n=1):
            a = BLOCK2_AT[name][0] + i
            return cols[:, a:a + n]

        def row(name):
            a, n = ROW_AT[name]
            return rows_sb[:, a:a + n]

        place = [0]

        def region(n):
            place[0] += n
            assert place[0] <= WORK, place
            return work[:, place[0] - n:place[0]]

        def rows(n, t=T):
            return region(n * t).rearrange("p (c t) -> p c t", t=t)

        proj = rows(len(PROJ))
        vtok = rows(TB, MIX)
        mixer_start = place[0]
        kc = rows(HEADS)
        qc = rows(HEADS)
        vmla = rows(TB, MIX)
        score = rows(2)
        probs = rows(2)
        probs_t = region(2 * TB * T).rearrange("p (r s t) -> p r s t", s=TB, t=T)
        negmax, rsum = region(16), region(16)
        turned = rows(2)
        place[0] = mixer_start
        cpos = rows(2)
        khat = region(4 * P).rearrange("p (d r s) -> p d r s", d=2, r=2)
        qhat = region(4 * T).rearrange("p (d r t) -> p d r t", d=2, r=2)
        qdiag = region(2 * HEADS * T).rearrange("p (d j n) -> p d j n", d=2, j=TB)
        kdec = region(2 * NSUB * P).rearrange("p (d i s) -> p d i s", d=2, i=NSUB)
        amat23 = region(2 * TB * T).rearrange("p (h j t) -> p h j t", h=2, j=TB)
        amat01 = sq[:].rearrange("p (h j) t -> p h j t", h=2)
        spare = lambda name: proj[:, SLOT[name]:SLOT[name] + 2, :]
        z_la, cneg, e_la, dtmp = spare("c0"), spare("h0"), spare("cq0"), spare("gate0")
        yn = proj[:, 0:KD, :]
        place[0] = 0
        act_ff = rows(KF)
        ubuf = rows(4, T + 2)
        cbuf = rows(4)
        gbuf = rows(2)
        y = xT
        place[0] = 0
        xtok = rows(TB, SSD_W)
        btok = rows(TB, GROUPS * P)
        y_start = place[0]
        xctx = rows(CB, SSD_W)
        bctx = rows(CB, GROUPS * P)
        place[0] = y_start
        ytok = rows(TB, SSD_W)
        states = rows(2, SSD_W)
        xw, xs = region(SSD_W), region(SSD_W)
        seg_at = place[0]
        seg_in = rows(2, HPG * P)
        seg = rows(2, HPG * P)
        cbm = rows(1, GROUPS * P)[:, 0, :]
        dt_raw, dt, la, cs, ecs, etot = (rows(NB, DT_W) for _ in range(6))
        wdec = dt_raw
        yoffs = turn_tables[:, :, 0:GW]
        rs_tok = sb("rs_tok", [P, TB])
        b_t = sq[:, 0:GROUPS, :]
        c_t = sq[:, GROUPS:2 * GROUPS, :]
        hc = work[:, seg_at:seg_at + KD * CTX].rearrange("p (k t) -> p k t", t=CTX)
        conv_x = xw[:, 0:2 * T].rearrange("p (r t) -> p r t", t=T)
        conv_c = xs[:, 0:2 * CTX].rearrange("p (r t) -> p r t", t=CTX)
        pad_x = padc[:].rearrange("p a t -> p (a t)")[:, 0:2 * (T + 4)].rearrange("p (r t) -> p r t", t=T + 4)
        pad_c = pads[:].rearrange("p a t -> p (a t)")[:, 0:2 * (CTX + 4)].rearrange("p (r t) -> p r t", t=CTX + 4)
        zs = xw[:, 0:2 * T].rearrange("p (r t) -> p r t", t=T)
        sumsq = sb("sumsq", [P, TB])
        mixed = work[:, 0:(XC + 4) * T].rearrange("p (c t) -> p c t", t=T)
        pool_in = states[:, 0, 0:2 * GRID_ROWS * 80].rearrange("p (r g t) -> p r g t", r=2, g=GRID_ROWS)
        pool_s = states[:, 1, 0:2 * GRID_ROWS * 80].rearrange("p (r g t) -> p r g t", r=2, g=GRID_ROWS)
        pooled = xs[:, 0:2 * T].rearrange("p (r t) -> p r t", t=T)

        def squares(width):
            if width == T:
                return sq[:]
            return sq[:, 0:KD * width // T, :].rearrange("p k t -> p (k t)").rearrange("p (k t) -> p k t", t=width)

        def amat(h):
            return (amat01 if h < 2 else amat23)[:, h % 2]

        place[0] = 0

        def parts(name, n, t):
            region(n * t)
            return nc.alloc_sbuf_tensor_at(name, [P, n, t], F32R, offset=work_at + 4 * (place[0] - n * t))

        h2_hi, h2_lo = parts("h2_hi", TB, D), parts("h2_lo", TB, D)
        pick = parts("pick", TB, P)
        xg_hi, xg_lo = parts("xg_hi", KD, P), parts("xg_lo", KD, P)
        act_hi, act_lo = parts("act_hi", KD, P), parts("act_lo", KD, P)
        w_hi = nc.alloc_sbuf_tensor_at("w_hi", [P, SPLITS, TILE], F32R, offset=x_at)
        w_lo = nc.alloc_sbuf_tensor_at("w_lo", [P, SPLITS, TILE], F32R, offset=x_at + 4 * SPLITS * TILE)
        pick_gate = rows(TB, P)
        gate_t = region(T)
        hb = region(2 * D)
        slots = padc[:, 0, 0:2 * P].rearrange("p (r s) -> p r s", s=P)
        picked = pads[:, 0, 0:4 * TB].rearrange("p (r b) -> p r b", b=TB)
        g_part, u_part, sig = region(D), region(D), region(D)
        y_slot = region(D)
        e_bias = region(3 * D)
        iota = region(T)
        logits = rows(TB, EXPERTS + TOP_K)
        marked = rows(TB, EXPERTS + TOP_K)
        top8, sought = rows(TB, 8), rows(TB, 8)
        chosen, gate, rank = rows(TB, EXPERTS), rows(TB, EXPERTS), rows(TB, EXPERTS)
        gate_sum = region(TB)
        n_blk, blk_end, above = region(EXPERTS), region(EXPERTS), region(EXPERTS)
        of_block = hb[:, 0:(MAX_BLOCKS + 1) * EXPERTS].rearrange("p (b e) -> p b e", e=EXPERTS)
        table_f = rows(3, MAX_BLOCKS + 1)
        table = rows(3, MAX_BLOCKS + 1).bitcast(I32)

        block = ctx.enter_context(nc.Block())

        def blocks_of(eng):
            return eng.value_load(table[0:1, 2, 0:1], min_val=1, max_val=MAX_BLOCKS)

        def when(*name):
            return marks[name][1] if marks is not None else 1

        def reached(*name):
            return (sems[marks[name][0]], marks[name][1]) if marks is not None else (pe_done, 1)

        def in_turn(i, *name, back=0):
            key, count = marks[("moe",) + name] if marks is not None else ("pe", 1)
            return i * per_turn(key) + (per_turn(key) * (1 - back) + count)

        def own_turn(i, did):
            return i * per_turn(did.key) + (per_turn(did.key) + did.n)

        def per_turn(key):
            return marks[("per_turn", key)][1] if marks is not None else 64

        def bank_of(*name):
            return banks[marks[("bank",) + name][1] if marks is not None else 0]

        @block.sync
        def _(sp):
            sp.dma_start(consts[:], io["consts"]).then_inc(s_in, 16)
            sp.dma_start(cols[:], io["cols"]).then_inc(s_in, 16)
            sp.dma_start(xT[:], io["x"].rearrange("p (k t) -> p k t", t=T)).then_inc(s_in, 16)
            sp.dma_start(pos_i[64:96, :], io["positions"].to_broadcast([32, T])).then_inc(s_in, 16)
            sp.dma_start(rows_sb[:], io["rows"].to_broadcast([P, NROWS])).then_inc(s_in, 16)
            n_tiles = io["wstream"].shape[0]
            for r in range(RING):
                sp.dma_start(ring[:, r, :], io["wstream"][r]).then_inc(s_tile[r], 16)
            with sp.Fori(1, n_tiles // RING) as g:
                for r in range(RING):
                    src = io["wstream"][bass.ds(g * RING + r, 1)].rearrange("a p n -> p (a n)")
                    sp.wait_ge(s_used, g * RING + (r + 1 - RING))
                    sp.dma_start(ring[:, r, :], src).then_inc(s_tile[r], 16)
            sp.wait_ge(dve_done, when("table"))
            with sp.Fori(0, blocks_of(sp)) as i:
                e = sp.value_load(table[0:1, 0, bass.ds(i, 1)], min_val=0, max_val=EXPERTS - 1)
                for t in range(MOE_TILES):
                    if t < 2 * KD:
                        src = io["w1"][bass.ds(e * KD + t // 2, 1)].rearrange("a p n -> p (a n)")
                        src = src[:, t % 2 * TILE:(t % 2 + 1) * TILE]
                    else:
                        src = io["w2"][bass.ds(e * KD + t - 2 * KD, 1)].rearrange("a p n -> p (a n)")
                    sp.wait_ge(s_used, i * MOE_TILES + (n_tiles + t + 1 - RING))
                    sp.dma_start(ring[:, t % RING, :], src).then_inc(s_tile[t % RING], 16)
                    if t == RING - 1:
                        b1 = io["b1"][bass.ds(e, 1), :].to_broadcast([P, 2 * D])
                        b2 = io["b2"][bass.ds(e, 1), :].to_broadcast([P, D])
                        sp.wait_ge(moe_dve_done, in_turn(i, "y_kept", 1, back=1))
                        sp.dma_start(e_bias[:, 0:2 * D], b1).then_inc(s_bias, 16)
                        sp.dma_start(e_bias[:, 2 * D:], b2).then_inc(s_bias, 16)
            sp.wait_ge(dve_done, when("normed", ("final",), KD - 1))
            sp.dma_start(io["out"].rearrange("p (k t) -> p k t", t=T), xT[:]).then_inc(s_out, 16)
            sp.wait_ge(s_out, 16)

        @block.gpsimd
        def _(pool):
            pool.wait_ge(pe_done, when("full", "mix", DEPTH - 1, KD - 1))
            pool.dma_start(hc, io["ctx"].rearrange("p (k t) -> p k t", t=CTX)).then_inc(s_ctx, 16)
            pool.wait_ge(pe_done, when("full", "out2", KD - 1))
            pool.dma_start(iota, io["iota"]).then_inc(s_iota, 16)
            pool.wait_ge(s_iota, 16)
            pool.wait_ge(act_done, when("first_xg_hi", 1))
            with pool.Fori(0, blocks_of(pool)) as i:
                turn_did = Count("pool", found, ("moe",))
                e = pool.value_load(table[0:1, 0, bass.ds(i, 1)], min_val=0, max_val=EXPERTS - 1)
                j = pool.value_load(table[0:1, 1, bass.ds(i, 1)], min_val=0, max_val=TB - 1)
                e_next = pool.value_load(table[0:1, 0, bass.ds(i + 1, 1)], min_val=0, max_val=EXPERTS - 1)
                j_next = pool.value_load(table[0:1, 1, bass.ds(i + 1, 1)], min_val=0, max_val=TB - 1)
                nc.gpsimd.tensor_copy(slots[:, 0, :], iota[:, bass.ds(j * P, P)]).then_inc(moe_pool_done,
                    turn_did.up())
                nc.gpsimd.tensor_copy(slots[:, 1, :], iota[:, bass.ds(j_next * P, P)]).then_inc(moe_pool_done,
                    turn_did.up())
                nc.gpsimd.tensor_copy(picked[:, 0, :].unsqueeze(2), rank[:, :, bass.ds(e,
                    1)]).then_inc(moe_pool_done, turn_did.up())
                nc.gpsimd.tensor_copy(picked[:, 1, :].unsqueeze(2), rank[:, :, bass.ds(e_next,
                    1)]).then_inc(moe_pool_done, turn_did.up())
                nc.gpsimd.tensor_copy(picked[:, 2, :].unsqueeze(2), gate[:, :, bass.ds(e,
                    1)]).then_inc(moe_pool_done, turn_did.up())
                pool.wait_ge(moe_pool_done, own_turn(i, turn_did))
                pool.wait_ge(moe_pe_done, in_turn(i, "gate_t", back=1))
                pool.wait_ge(moe_pe_done, in_turn(i, "xg", 1, back=1))
                nc.gpsimd.tensor_tensor(picked[:, 3, :], picked[:, 2, :], const("ones")[:, 0:TB],
                    ALU.mult).then_inc(moe_pool_done, turn_did.up())
                for b in range(TB):
                    nc.gpsimd.tensor_scalar(pick[:, b, :], slots[:, 1, :], picked[:, 1, b:b + 1], None,
                        ALU.is_equal).then_inc(moe_pool_done, turn_did.up(("pick",)))
                for b in range(TB):
                    nc.gpsimd.tensor_scalar(pick_gate[:, b, :], slots[:, 0, :], picked[:, 0, b:b + 1], None,
                        ALU.is_equal).then_inc(moe_pool_done, turn_did.up())
                pool.wait_ge(moe_pool_done, own_turn(i, turn_did))
                for b in range(TB):
                    nc.gpsimd.tensor_tensor(pick_gate[:, b, :], pick_gate[:, b, :], picked[:, 3,
                        b:b + 1].to_broadcast([P, P]), ALU.mult).then_inc(moe_pool_done, turn_did.up(("pick_gate",)))
                pool.wait_ge(moe_pool_done, own_turn(i, turn_did))
                turn_did.close()

        @block.tensor
        def _(pe):
            did = Count("pe", found)
            state = {"job": 0, "tile": 0, "pending": 0}
            holder = [None] * 8

            def bank(*name):
                b = state["job"] % 8
                state["job"] += 1
                if holder[b] is not None:
                    pe.wait_ge(*reached("free", *holder[b]))
                holder[b] = name
                found[("bank",) + name] = ("bank", b)
                return banks[b]

            def mm(out, l, r, start, stop, *full):
                ins = nc.tensor.matmul(out, l, r, start=start, stop=stop)
                if full:
                    ins.then_inc(pe_done, did.up(("full",) + full))
                elif state["pending"]:
                    ins.then_inc(s_used, state["pending"])
                    state["pending"] = 0

            def tile():
                n = state["tile"]
                state["tile"] += 1
                pe.wait_ge(s_tile[n % RING], 16 * (n // RING + 1))
                return ring[:, n % RING, :]

            def used(n=1):
                state["pending"] += n

            def chunks(name, lhs, rhs, n, m=P, width=T):
                out = bank(*name)
                for k in range(n):
                    mm(out[0:m, 0:width], lhs(k), rhs(k), k == 0, k == n - 1, *(name if k == n - 1 else ()))

            def norm(tag, src, at, n, ones, center=True, width=T):
                if center:
                    pe.wait_ge(dve_done, when("norm_in", tag))
                    chunks(("mean", tag), lambda k: ones, lambda k: src[:, k, :], n)
                for k in range(n):
                    pe.wait_ge(act_done, when("square", tag, k))
                chunks(("var", tag), lambda k: ones, lambda k: squares(width)[:, at + k, :], n, width=width)

            def project(name):
                w = tile().rearrange("p (k m) -> p k m", m=P)
                chunks(name, lambda k: w[:, k, :], lambda k: hT[:, k, :], KD)
                used()

            pe.wait_ge(s_in, 16 * 5)
            ident, ones, ones_mix, ones_d = const("ident"), const("ones"), const("ones_mix"), const("ones_d")
            norm(("in",), xT, 0, KD, ones_d)
            for l in range(DEPTH):
                pe.wait_ge(act_done, when("norm_out", ("in",) if l == 0 else ("ln2", l - 1), KD - 1))
                for name in PROJ[:4]:
                    project(("proj", l, name))
                w = tile().rearrange("p (k m) -> p k m", m=P)
                chunks(("proj", l, "misc"), lambda k: w[:, k, :], lambda k: hT[:, k, :], KD)
                chunks(("kswap", l), lambda k: w[:, k, 32:128], lambda k: hT[:, k, :], KD, 96)
                used()
                for name in PROJ[5:10]:
                    project(("proj", l, name))
                w0 = tile().rearrange("p (k m) -> p k m", m=MIX)
                w1 = tile().rearrange("p (k m) -> p k m", m=MIX)
                for b in range(TB):
                    out = bank("gv", l, b)
                    for k in range(KD):
                        mm(out[:, 0:MIX], hT[:, k, b * P:(b + 1) * P], (w0 if k < 4 else w1)[:, k % 4, :],
                           k == 0, k == KD - 1, *(("gv", l, b) if k == KD - 1 else ()))
                used(2)
                for name in PROJ[10:]:
                    project(("proj", l, name))
                wq = tile().rearrange("p (k n) -> p k n", k=2)
                wkv = tile()
                norm(("kv", l), sq, 0, 1, ones, center=False)
                norm(("q", l), sq, 1, 2, ones_mix, center=False)
                ckv, cq = proj[:, SLOT["ckv"], :], proj[:, SLOT["cq0"]:SLOT["cq0"] + 2, :]
                pe.wait_ge(dve_done, when("normed", ("kv", l), 0))
                for h in range(HEADS):
                    chunks(("knope", l, h), lambda k: wkv[:, h * NOPE:(h + 1) * NOPE], lambda k: ckv, 1, NOPE)
                for b in range(TB):
                    mm(bank("mv", l, b)[:, 0:MIX], ckv[:, b * P:(b + 1) * P], wkv[:, MIX:2 * MIX], True, True,
                       "mv", l, b)
                pe.wait_ge(dve_done, when("normed", ("q", l), 1))
                for h in range(HEADS):
                    chunks(("qh", l, h), lambda k: wq[:, k, h * P:h * P + 96], lambda k: cq[:, k, :], 2, 96)
                    chunks(("qswap", l, h), lambda k: wq[:, k, h * P + 32:h * P + P], lambda k: cq[:, k, :], 2, 96)
                for d in range(2):
                    chunks(("la", l, d), lambda k: wkv[0:32, 2 * MIX + d * P:2 * MIX + (d + 1) * P],
                           lambda k: proj[0:32, SLOT["misc"], :], 1)
                used(2)

                def scores(i):
                    pe.wait_ge(dve_done, when("query", l, i // TB))
                    chunks(("score", l, i), lambda k: qc[0:96, i // TB, i % TB * P:(i % TB + 1) * P],
                           lambda k: kc[0:96, i // TB, :], 1)

                def values(name, vals, probs_of, h):
                    o = DV * (h % 2)
                    out = bank(*name)
                    for s in range(TB):
                        mm(out[o:o + DV, :], vals[:, s, h * DV:(h + 1) * DV], probs_of(s), s == 0, s == TB - 1,
                           *(name if s == TB - 1 else ()))

                pe.wait_ge(dve_done, when("keys", l))
                pe.wait_ge(act_done, when("key_nope", l, HEADS - 1))
                pe.wait_ge(act_done, when("mv_kept", l, TB - 1))
                scores(0)
                for i in range(HEADS * TB):
                    if i + 1 < HEADS * TB:
                        scores(i + 1)
                    pe.wait_ge(dve_done, when("probs", l, i))
                    out = bank("turn", l, i)
                    for s in range(TB):
                        ins = nc.tensor.transpose(out[:, s * P:(s + 1) * P], probs[:, i % 2, s * P:(s + 1) * P], ident)
                    ins.then_inc(pe_done, did.up(("full", "turn", l, i)))
                    if i % TB == TB - 1:
                        h = i // TB
                        pe.wait_ge(act_done, when("turned", l, i))
                        values(("yc", l, h), vmla, lambda s: probs_t[:, h % 2, s, :], h)
                for j in range(TB):
                    for d in range(2):
                        pe.wait_ge(dve_done, when("kdec", l, j, d))
                        out = bank("gdiag", l, j, d)
                        for i in range(NSUB):
                            mm(out[:, i * 64:(i + 1) * 64], kdec[:, d, i, :], qdiag[:, d, j, i * 64:(i + 1) * 64],
                               True, True, *(("gdiag", l, j, d) if i == NSUB - 1 else ()))
                    for d in range(2):
                        if 0 < (TB - 1 - j, j)[d]:
                            pe.wait_ge(dve_done, when("qhat", l, j, d))
                    for h in range(HEADS):
                        out = bank("goff", l, j, h)
                        hp = slice(DK * h, DK * (h + 1))
                        if j > 0:
                            mm(out[:, 0:j * P], khat[hp, 1, j % 2, :], qhat[hp, 1, j % 2, 0:j * P], True, True,
                               *(("goff", l, j, h) if j == TB - 1 else ()))
                        if j < TB - 1:
                            mm(out[:, (j + 1) * P:T], khat[hp, 0, j % 2, :], qhat[hp, 0, j % 2, (j + 1) * P:T],
                               True, True, "goff", l, j, h)
                pe.wait_ge(dve_done, when("amat", l))
                for h in range(HEADS):
                    values(("yb", l, h), vtok, lambda s: amat(h)[:, s, :], h)
                for c in range(2):
                    norm(("gla", l, c), sq, c, 1, const("heads64"), center=False)
                norm(("cfm", l), proj, 0, 2, ones_mix)
                for b in range(4):
                    norm(("branch", l, b), sq, 2 * b, 2, ones_mix, center=False)
                for b in range(4):
                    pe.wait_ge(dve_done, when("normed", ("branch", l, b), 1))
                for m in range(KD):
                    w = tile().rearrange("p (k m) -> p k m", m=P)
                    chunks(("mix", l, m), lambda k: w[:, k, :], lambda k: yn[:, k, :], KD)
                    used()
                norm(("ln1", l), xT, 0, KD, ones_d)
                pe.wait_ge(act_done, when("norm_out", ("ln1", l), KD - 1))
                for c in range(KF):
                    project(("up", l, c, 0))
                    project(("up", l, c, 1))
                for m in range(KD):
                    out = bank("down", l, m)
                    for k in range(KF):
                        if k % 8 == 0:
                            w = tile().rearrange("p (k m) -> p k m", m=P)
                        if m == 0:
                            pe.wait_ge(dve_done, when("act_ff", l, k))
                        mm(out[:], w[:, k % 8, :], act_ff[:, k, :], k == 0, k == KF - 1,
                           *(("down", l, m) if k == KF - 1 else ()))
                        if k % 8 == 7 or k == KF - 1:
                            used()
                norm(("ln2", l), xT, 0, KD, ones_d)

            pe.wait_ge(act_done, when("csil"))
            out = bank("mod")
            for m in range(6 * KD):
                w = tile().rearrange("p (k m) -> p k m", m=P)
                for k in range(KD):
                    mm(out[:, 2 * m:2 * m + 2], w[:, k, :], csil[:, 2 * k:2 * k + 2], k == 0, k == KD - 1,
                       *(("mod",) if (m, k) == (6 * KD - 1, KD - 1) else ()))
                used()
            norm(("ctx1",), None, 0, KD, ones_d, center=False, width=CTX)
            norm(("x1",), None, 0, KD, ones_d, center=False)
            for k in range(KD):
                pe.wait_ge(act_done, when("norm_out", ("ctx1",), k))
                pe.wait_ge(act_done, when("norm_out", ("x1",), k))

            def turn(c):
                for kind, n, src in (("x", TB, conv_x[:, c % 2] if c < XC else b_t[:, c - XC]),
                                     ("c", CB, conv_c[:, c % 2])):
                    pe.wait_ge(act_done, when("conv_out", kind, c))
                    out = bank("tok", kind, c)
                    for b in range(n):
                        ins = nc.tensor.transpose(out[:, b * P:(b + 1) * P], src[:, b * P:(b + 1) * P], ident)
                    ins.then_inc(pe_done, did.up(("full", "tok", kind, c)))

            w = tile().rearrange("p (k m) -> p k m", m=P)
            out = bank("dt")
            for b in range(NB):
                src, o = (xT, b * P) if b < TB else (hc, (b - TB) * P)
                for k in range(KD):
                    mm(out[:, b * DT_W:(b + 1) * DT_W], src[:, k, o:o + P], w[:, k, 0:DT_W], k == 0, k == KD - 1,
                       *(("dt",) if (b, k) == (NB - 1, KD - 1) else ()))
            used()
            for c in range(XC + 2 * GROUPS):
                w = tile().rearrange("p (k m) -> p k m", m=P)
                chunks(("chan", "x", c), lambda k: w[:, k, :], lambda k: xT[:, k, :], KD)
                if c < XC + GROUPS:
                    chunks(("chan", "c", c), lambda k: w[:, k, :], lambda k: hc[:, k, :], KD, width=CTX)
                used()
                if 1 <= c <= XC + GROUPS:
                    turn(c - 1)
            pe.wait_ge(dve_done, when("la"))
            out = bank("cs")
            for b in range(NB):
                for d, tri in enumerate((const("upto"), const("from"))):
                    a = b * DT_W + d * SSD_HEADS
                    mm(out[:, a:a + SSD_HEADS], tri, la[:, b, d * SSD_HEADS:(d + 1) * SSD_HEADS], True, True,
                       *(("cs",) if (b, d) == (NB - 1, 1) else ()))
            mm(bank("total")[:, 0:NB * DT_W], ones, la.rearrange("p b n -> p (b n)"), True, True, "total")
            pe.wait_ge(act_done, when("conv_out", "x", XC + 2 * GROUPS - 1))
            for s, (d, kind, b) in enumerate(SCAN):
                if kind == "x":
                    c_of = lambda g: c_t[:, g, b * P:(b + 1) * P]
                    out = bank("cb", s)
                    for g in range(GROUPS):
                        mm(out[:, g * P:(g + 1) * P], b_t[:, g, b * P:(b + 1) * P], c_of(g), True, True,
                           *(("cb", s) if g == GROUPS - 1 else ()))

                    def segments(g):
                        pe.wait_ge(dve_done, when("seg_in", s, g))
                        for half in range(2):
                            mm(bank("seg", s, g, half)[:, 0:GW], const(("after", "before")[d]),
                               seg_in[:, g % 2, half * GW:(half + 1) * GW], True, True, "seg", s, g, half)

                    def within(g):
                        pe.wait_ge(dve_done, when("amat2", s, g))
                        out = bank("yd", s, g)
                        for e in range(HPG):
                            o = e * HEAD_W
                            mm(out[:, o:o + HEAD_W], seg[:, g % 2, e * P:(e + 1) * P], xs[:, g * GW + o:g * GW + o + HEAD_W],
                               True, True, *(("yd", s, g) if e == HPG - 1 else ()))

                    segments(0)
                    for g in range(GROUPS):
                        if g == 0:
                            pe.wait_ge(dve_done, when("state", SCAN_PREV[s]))
                        mm(bank("yoff", s, g)[:, 0:GW], c_of(g), states[:, d, g * GW:(g + 1) * GW], True, True,
                           "yoff", s, g)
                    pe.wait_ge(dve_done, when("xs", s))
                    for g in range(GROUPS):
                        if g + 1 < GROUPS:
                            segments(g + 1)
                        within(g)
                pe.wait_ge(dve_done, when("xw", s))
                for g in range(GROUPS):
                    src = (btok if kind == "x" else bctx)[:, b, g * P:(g + 1) * P]
                    mm(bank("st", s, g)[:, 0:GW], src, xw[:, g * GW:(g + 1) * GW], True, True, "st", s, g)
            for cg in range(SSD_W // 512):
                ws = [tile().rearrange("p (k n) -> p k n", n=512) for _ in range(4)]
                for b in range(TB):
                    out = bank("z", cg, b)
                    for k in range(KD):
                        mm(out[:], xT[:, k, b * P:(b + 1) * P], ws[k // 2][:, k % 2, :], k == 0, k == KD - 1,
                           *(("z", cg, b) if k == KD - 1 else ()))
                used(4)
            for g in range(4):
                w = tile().rearrange("p (k m) -> p k m", m=P)
                chunks(("pool", g), lambda k: w[:, k, :], lambda k: xT[:, k, :], KD)
                used()
            w = tile()
            for g in range(4):
                pe.wait_ge(dve_done, when("pooled", g))
                mm(bank("poolw", g)[:], w[:, g * P:(g + 1) * P], pooled[:, g % 2, :], True, True, "poolw", g)
            used()
            for b in range(TB):
                pe.wait_ge(dve_done, when("ynormed", b))
            for c in range(XC):
                out = bank("yt", c)
                for b in range(TB):
                    ins = nc.tensor.transpose(out[:, b * P:(b + 1) * P], ytok[:, b, c * P:(c + 1) * P], ident)
                ins.then_inc(pe_done, did.up(("full", "yt", c)))
            for m in range(KD):
                out = bank("out2", m)
                for k in range(XC + 4):
                    if k % 8 == 0:
                        w = tile().rearrange("p (k m) -> p k m", m=P)
                    if m == 0:
                        pe.wait_ge(act_done, when("mixed", k))
                    mm(out[:], w[:, k % 8, :], mixed[:, k, :], k == 0, k == XC + 3,
                       *(("out2", m) if k == XC + 3 else ()))
                    if k % 8 == 7:
                        used()

            norm(("x2",), None, 0, KD, ones_d, center=False)
            for k in range(KD):
                pe.wait_ge(act_done, when("norm_out", ("x2",), k))
            w = tile().rearrange("p (k m) -> p k m", m=P)
            out = bank("router")
            for b in range(TB):
                for k in range(KD):
                    mm(out[:, b * EXPERTS:(b + 1) * EXPERTS], xT[:, k, b * P:(b + 1) * P], w[:, k, 0:EXPERTS],
                       k == 0, k == KD - 1, *(("router",) if (b, k) == (TB - 1, KD - 1) else ()))
            used()
            for b in range(TB):
                for half in range(2):
                    out = bank("h2t", b, half)
                    for k in range(4):
                        ins = nc.tensor.transpose(out[:, k * P:(k + 1) * P],
                                                  xT[:, half * 4 + k, b * P:(b + 1) * P], ident)
                    ins.then_inc(pe_done, did.up(("full", "h2t", b, half)))
            pe.wait_ge(dve_done, when("chosen"))
            out = bank("rank")
            for b in range(TB + 1):
                for c in range(min(b + 1, TB)):
                    mm(out[:, b * EXPERTS:(b + 1) * EXPERTS], const("before") if c == b else ones, chosen[:, c, :],
                       c == 0, c == min(b, TB - 1), *(("rank",) if (b, c) == (TB, TB - 1) else ()))
            n_tiles = io["wstream"].shape[0]
            while state["tile"] < n_tiles:
                tile()
                used()
            for b in range(8):
                if holder[b] is not None:
                    pe.wait_ge(dve_done, when("free", *holder[b]))
                    holder[b] = None
            pe.wait_ge(s_iota, 16)
            nc.tensor.matmul(banks[0][:, 0:2], ident, ident[:, 0:2], start=True, stop=True)\
              .then_inc(s_used, state["pending"])
            due = [0]

            def gather(done):
                for k in range(KD):
                    out = banks[4 + k // 4][:, k % 4 * P:(k % 4 + 1) * P]
                    for b in range(TB):
                        ins = nc.tensor.matmul(out, h2_hi[:, b, k * P:(k + 1) * P], pick[:, b, :], start=b == 0,
                                               stop=False)
                        if due[0]:
                            ins.then_inc(s_freed, due[0])
                            due[0] = 0
                        ins = nc.tensor.matmul(out, h2_lo[:, b, k * P:(k + 1) * P], pick[:, b, :], start=False,
                                               stop=b == TB - 1)
                    if k % 4 == 3:
                        done(ins, k // 4)

            pe.wait_ge(dve_done, when("first_pick"))

            def first_done(ins, half):
                ins.then_inc(pe_done, did.up(("first_xg", half)))

            gather(first_done)
            pe.wait_ge(dve_done, when("table"))
            pe.wait_ge(dve_done, when("first_xg_kept"))
            with pe.Fori(0, blocks_of(pe)) as i:
                turn_did = Count("pe", found, ("moe",))
                due[0] = 1

                def lmm(out, l, r, start, stop, *names):
                    ins = nc.tensor.matmul(out, l, r, start=start, stop=stop)
                    if names:
                        ins.then_inc(moe_pe_done, turn_did.up(names))
                    elif due[0]:
                        ins.then_inc(s_freed, due[0])
                        due[0] = 0

                def product(t, left_hi, left_lo, out, k, *names):
                    pe.wait_ge(s_used, i * MOE_TILES + (n_tiles + t + 1))
                    hi, lo = w_hi[:, t % SPLITS, :], w_lo[:, t % SPLITS, :]
                    for p, (l, r) in enumerate(((left_hi, hi), (left_hi, lo), (left_lo, hi))):
                        for n in range(2):
                            lmm(out[n][:], l[:, k, :], r[:, n * 512:(n + 1) * 512], (k, p) == (0, 0),
                                (k, p) == (KD - 1, 2), *(names if (p, n) == (2, 1) else ()))
                    due[0] += 1

                def hidden(k):
                    for half in range(2):
                        product(2 * k + half, xg_hi, xg_lo, banks[2 * half:2 * half + 2], k,
                                *(("h",) if (k, half) == (KD - 1, 1) else ()))

                pe.wait_ge(moe_dve_done, in_turn(i, "xg_kept", 1, back=1))
                for k in range(KD // 2):
                    hidden(k)
                pe.wait_ge(moe_dve_done, in_turn(i, "y_kept", 1, back=1))
                for m in range(KD):
                    if m >= 4 and m % 2 == 0:
                        pe.wait_ge(moe_dve_done, in_turn(i, "acc", m - 3))
                    lmm(banks[BACK_BANK[m]][:], y_slot[:, m * P:(m + 1) * P], gate_t, True, True,
                        *(("back", m) if m % 2 else ()))
                for k in range(KD // 2, KD):
                    hidden(k)
                pe.wait_ge(moe_pool_done, in_turn(i, "pick"))
                pe.wait_ge(moe_dve_done, in_turn(i, "acc", 5))

                def xg_done(ins, half):
                    ins.then_inc(moe_pe_done, turn_did.up(("xg", half)))

                gather(xg_done)
                pe.wait_ge(moe_dve_done, in_turn(i, "acc", KD - 1))
                pe.wait_ge(moe_dve_done, in_turn(i, "act"))
                for k in range(KD):
                    ins = nc.tensor.transpose(banks[6 + k // 4][:, k % 4 * P:(k % 4 + 1) * P],
                                              u_part[:, k * P:(k + 1) * P], ident)
                    if k % 4 == 3:
                        ins.then_inc(moe_pe_done, turn_did.up(("act_t", k // 4)))
                pe.wait_ge(moe_pool_done, in_turn(i, "pick_gate"))
                for b in range(TB):
                    ins = nc.tensor.transpose(banks[0][:, b * P:(b + 1) * P], pick_gate[:, b, :], ident)
                ins.then_inc(moe_pe_done, turn_did.up(("gate_t",)))
                pe.wait_ge(moe_dve_done, in_turn(i, "xg_kept", 1))
                pe.wait_ge(moe_dve_done, in_turn(i, "act_t_kept", 1))
                for k in range(KD):
                    product(2 * KD + k, act_hi, act_lo, banks[4:6], k, *(("y",) if k == KD - 1 else ()))
                pe.wait_ge(moe_act_done, in_turn(i, "gate_t_kept"))
                turn_did.close()
            pe.wait_ge(dve_done, when("last_y_kept"))
            for m in range(KD):
                if m >= 4:
                    pe.wait_ge(dve_done, when("last_acc", m - 4))
                nc.tensor.matmul(banks[BACK_BANK[m]][:], y_slot[:, m * P:(m + 1) * P], gate_t, start=True,
                    stop=True).then_inc(pe_done, did.up(("last_back", m)))
            norm(("final",), None, 0, KD, ones_d, center=False)

        @block.scalar
        def _(act):
            did = Count("act", found)
            norms = []


            def deviation(tag, eps="eps", width=T, scale=1.0):
                if len(norms) >= 2:
                    act.wait_ge(dve_done, when("normed_all", norms[-2]))
                out = rstd[:, len(norms) % 2, 0:width]
                norms.append(tag)
                act.wait_ge(pe_done, when("full", "var", tag))
                act.wait_ge(act_done, did.n)
                nc.scalar.activation(out, bank_of("var", tag)[:, 0:width], ACT.Sqrt, bias=const(eps),
                    scale=scale).then_inc(act_done, did.up(("free", "var", tag), ("deviation", tag)))

            def layer_norm(tag, src, n):
                for k in range(n):
                    act.wait_ge(dve_done, when("centred", tag, k))
                    act.wait_ge(act_done, did.n)
                    nc.scalar.activation(sq[:, k, :], src[:, k, :], ACT.Square).then_inc(act_done, did.up(("square",
                        tag, k)))
                deviation(tag)

            def shifted(tag, src, dst, n, bcol, func=ACT.Identity):
                for k in range(n):
                    act.wait_ge(dve_done, when("normed", tag, k))
                    act.wait_ge(act_done, did.n)
                    nc.scalar.activation(dst[:, k, :], src[:, k, :], func, bias=bcol(k)).then_inc(act_done,
                        did.up(("norm_out", tag, k)))

            act.wait_ge(s_in, 16 * 5)
            act.wait_ge(dve_done, when("angles"))
            act.wait_ge(act_done, did.n)
            nc.scalar.activation(sin_t[64:96, :], sin_t[64:96, :], ACT.Sin).then_inc(act_done, did.up())
            act.wait_ge(act_done, did.n)
            nc.scalar.activation(cos_t[64:96, :], cos_t[64:96, :], ACT.Sin).then_inc(act_done, did.up(("sines",)))
            layer_norm(("in",), xT, KD)
            shifted(("in",), xT, hT, KD, lambda k: col(None, "ln_in_b", k))
            for l in range(DEPTH):
                def keep(name, func=ACT.Copy, **kw):
                    act.wait_ge(pe_done, when("full", "proj", l, name))
                    act.wait_ge(act_done, did.n)
                    nc.scalar.activation(proj[:, SLOT[name], :], bank_of("proj", l, name)[:], func,
                        **kw).then_inc(act_done, did.up(("free", "proj", l, name), ("proj", l, name)))

                keep("a0"), keep("a1"), keep("gate0", ACT.Sigmoid), keep("gate1", ACT.Sigmoid)
                keep("misc")
                for i, name in enumerate(("ckv", "cq0", "cq1")):
                    tag, k = (("kv", l), 0) if i == 0 else (("q", l), i - 1)
                    act.wait_ge(pe_done, when("full", "proj", l, name))
                    act.wait_ge(act_done, did.n)
                    nc.scalar.activation(sq[:, i, :], bank_of("proj", l, name)[:], ACT.Square).then_inc(act_done,
                        did.up(("square", tag, k)))
                    keep(name)
                act.wait_ge(pe_done, when("full", "proj", l, "q"))
                act.wait_ge(act_done, did.n)
                nc.scalar.activation(proj[:, SLOT["q"], :], bank_of("proj", l, "q")[:], ACT.Copy,
                    scale=DK ** -0.5).then_inc(act_done, did.up(("free", "proj", l, "q"), ("proj", l, "q")))
                keep("k")
                for b in range(TB):
                    act.wait_ge(pe_done, when("full", "gv", l, b))
                    act.wait_ge(act_done, did.n)
                    nc.scalar.activation(vtok[:, b, :], bank_of("gv", l, b)[:, 0:MIX], ACT.Copy).then_inc(act_done,
                        did.up(("free", "gv", l, b), ("gv_kept", l, b)))
                for name in PROJ[10:16]:
                    keep(name)
                keep("gg0", ACT.Silu), keep("gg1", ACT.Silu)
                deviation(("kv", l), scale=1.0 / P)
                deviation(("q", l))
                for h in range(HEADS):
                    act.wait_ge(pe_done, when("full", "knope", l, h))
                    act.wait_ge(act_done, did.n)
                    nc.scalar.activation(kc[0:NOPE, h, :], bank_of("knope", l, h)[0:NOPE, :],
                        ACT.Copy).then_inc(act_done, did.up(("free", "knope", l, h), ("key_nope", l, h)))
                for b in range(TB):
                    act.wait_ge(pe_done, when("full", "mv", l, b))
                    act.wait_ge(act_done, did.n)
                    nc.scalar.activation(vmla[:, b, :], bank_of("mv", l, b)[:, 0:MIX], ACT.Copy).then_inc(act_done,
                        did.up(("free", "mv", l, b), ("mv_kept", l, b)))
                scale = (NOPE + ROPE) ** -0.5

                def turned_out(i):
                    h, b = i // TB, i % TB
                    act.wait_ge(pe_done, when("full", "turn", l, i))
                    act.wait_ge(act_done, did.n)
                    nc.scalar.activation(probs_t[:, h % 2, :, b * P:(b + 1) * P], bank_of("turn", l,
                        i)[:].rearrange("p (s t) -> p s t", t=P), ACT.Copy).then_inc(act_done, did.up(("free",
                        "turn", l, i), ("turned", l, i)))
                    if b == TB - 1:
                        o = DV * (h % 2)
                        act.wait_ge(pe_done, when("full", "yc", l, h))
                        act.wait_ge(act_done, did.n)
                        nc.scalar.activation(y[o:o + DV, 4 + h // 2, :], bank_of("yc", l, h)[o:o + DV, :],
                            ACT.Copy).then_inc(act_done, did.up(("free", "yc", l, h), ("yc", l, h)))

                for i in range(HEADS * TB):
                    if i >= 2:
                        act.wait_ge(pe_done, when("full", "turn", l, i - 2))
                    act.wait_ge(pe_done, when("full", "score", l, i))
                    act.wait_ge(act_done, did.n)
                    nc.scalar.activation(score[:, i % 2, :], bank_of("score", l, i)[:], ACT.Copy,
                        scale=scale).then_inc(act_done, did.up(("free", "score", l, i), ("score_kept", l, i)))
                    act.wait_ge(dve_done, when("negmax", l, i))
                    act.wait_ge(act_done, did.n)
                    nc.scalar.activation(probs[:, i % 2, :], score[:, i % 2, :], ACT.Exp, bias=negmax[:, i:i + 1],
                        accum_out=rsum[:, i:i + 1]).then_inc(act_done, did.up(("exps", l, i)))
                    if i >= 1:
                        turned_out(i - 1)
                turned_out(HEADS * TB - 1)
                for d in range(2):
                    act.wait_ge(dve_done, when("la_abs", l, d))
                    act.wait_ge(act_done, did.n)
                    nc.scalar.activation(e_la[:, d, :], e_la[:, d, :], ACT.Exp, scale=-1.0).then_inc(act_done,
                        did.up())
                act.wait_ge(act_done, did.n)
                for d in range(2):
                    act.wait_ge(act_done, did.n)
                    nc.scalar.activation(e_la[:, d, :], e_la[:, d, :], ACT.Ln, bias=const("ones")[:,
                        0:1]).then_inc(act_done, did.up(("la_log", l, d)))
                act.wait_ge(dve_done, when("qdiag_arg", l))
                for d in range(2):
                    act.wait_ge(act_done, did.n)
                    nc.scalar.activation(z_la[:, d, :], z_la[:, d, :], ACT.Exp).then_inc(act_done,
                        did.up(("qdiag_exp", l, d)))
                for j in range(TB):
                    for d in range(2):
                        if j > 0:
                            act.wait_ge(pe_done, when("full", "gdiag", l, j - 1, d))
                        for i in range(NSUB):
                            a = j * P + i * SUB + (0, SUB - 1)[d]
                            s0, s1 = ((0, (i + 1) * SUB), (i * SUB, P))[d]
                            act.wait_ge(act_done, did.n)
                            nc.scalar.activation(kdec[:, d, i, s0:s1], cpos[:, d, j * P + s0:j * P + s1], ACT.Exp,
                                bias=cpos[:, d, a:a + 1], scale=-1.0).then_inc(act_done, did.up(*([("kdec_exp", l, j,
                                d)] if i == NSUB - 1 else [])))
                    for d in range(2):
                        if 0 < (TB - 1 - j, j)[d]:
                            a = (j * P + P - 1, j * P)[d]
                            t0, t1 = (((j + 1) * P, T), (0, j * P))[d]
                            if j >= 2:
                                act.wait_ge(pe_done, when("full", "goff", l, j - 2, HEADS - 1))
                            act.wait_ge(act_done, did.n)
                            nc.scalar.activation(khat[:, d, j % 2, :], cpos[:, d, j * P:(j + 1) * P], ACT.Exp,
                                bias=cpos[:, d, a:a + 1], scale=-1.0).then_inc(act_done, did.up())
                            act.wait_ge(act_done, did.n)
                            nc.scalar.activation(qhat[:, d, j % 2, t0:t1], cpos[:, d, t0:t1], ACT.Exp, bias=cneg[:,
                                d, a:a + 1]).then_inc(act_done, did.up(("qhat_exp", l, j, d)))
                    for h in range(HEADS):
                        act.wait_ge(pe_done, when("full", "goff", l, j, h))
                        src = bank_of("goff", l, j, h)
                        if j > 0:
                            act.wait_ge(act_done, did.n)
                            nc.scalar.activation(amat(h)[:, j, 0:j * P], src[:, 0:j * P],
                                ACT.Copy).then_inc(act_done, did.up(*([("free", "goff", l, j,
                                h)] if j == TB - 1 else [])))
                        if j < TB - 1:
                            act.wait_ge(act_done, did.n)
                            nc.scalar.activation(amat(h)[:, j, (j + 1) * P:T], src[:, (j + 1) * P:T],
                                ACT.Copy).then_inc(act_done, did.up(("free", "goff", l, j, h)))
                did.note("amat_off", l)
                for h in range(HEADS):
                    o = DV * (h % 2)
                    act.wait_ge(pe_done, when("full", "yb", l, h))
                    src = bank_of("yb", l, h)
                    act.wait_ge(act_done, did.n)
                    nc.scalar.activation(proj[o:o + DV, SLOT["b0"] + h // 2, :], src[o:o + DV, :],
                        ACT.Copy).then_inc(act_done, did.up(("free", "yb", l, h)))
                act.wait_ge(act_done, did.n)
                for c in range(2):
                    act.wait_ge(act_done, did.n)
                    nc.scalar.activation(sq[:, c, :], proj[:, SLOT["b0"] + c, :], ACT.Square).then_inc(act_done,
                        did.up(("square", ("gla", l, c), 0)))
                for c in range(2):
                    deviation(("gla", l, c))
                layer_norm(("cfm", l), proj, 2)
                shifted(("cfm", l), proj, y[:, 6:8, :], 2, lambda k: col(l, "cfm_b", k), ACT.Silu)
                for b, ready in enumerate((("ya", l), ("yb_gated", l), None, None)):
                    if ready:
                        act.wait_ge(dve_done, when(*ready))
                    else:
                        act.wait_ge(act_done, did.n)
                    for k in range(2):
                        act.wait_ge(act_done, did.n)
                        nc.scalar.activation(sq[:, 2 * b + k, :], y[:, 2 * b + k, :], ACT.Square).then_inc(act_done,
                            did.up(("square", ("branch", l, b), k)))
                for b in range(4):
                    deviation(("branch", l, b))
                layer_norm(("ln1", l), xT, KD)
                shifted(("ln1", l), xT, hT, KD, lambda k: col(l, "ln1_b", k))

                def gated(c):
                    act.wait_ge(dve_done, when("conv_ff", l, c, 0))
                    if c >= 2:
                        act.wait_ge(dve_done, when("act_ff", l, c - 2))
                    act.wait_ge(act_done, did.n)
                    nc.scalar.activation(gbuf[:, c % 2, :], cbuf[:, 2 * c % 4, :], ACT.Silu).then_inc(act_done,
                        did.up(("silu_ff", l, c)))

                act.wait_ge(dve_done, when("pads_ff", l))
                for c in range(KF):
                    for v in range(2):
                        i = 2 * c + v
                        if i >= 4:
                            act.wait_ge(dve_done, when("conv_ff", l, c - 2, v))
                        act.wait_ge(pe_done, when("full", "up", l, c, v))
                        act.wait_ge(act_done, did.n)
                        nc.scalar.activation(ubuf[:, i % 4, 1:T + 1], bank_of("up", l, c, v)[:],
                            ACT.Copy).then_inc(act_done, did.up(("free", "up", l, c, v), ("up_kept", l, c, v)))
                    if c >= 1:
                        gated(c - 1)
                gated(KF - 1)
                layer_norm(("ln2", l), xT, KD)
                shifted(("ln2", l), xT, hT, KD, lambda k: col(l, "ln2_b", k))

            act.wait_ge(act_done, did.n)
            nc.scalar.activation(csil[:], col2("cond", 0, 16), ACT.Silu).then_inc(act_done, did.up(("csil",)))
            act.wait_ge(s_ctx, 16)
            for tag, src, width in ((("ctx1",), hc, CTX), (("x1",), hT, T)):
                if width == T:
                    act.wait_ge(pe_done, when("full", "var", ("ctx1",)))
                for k in range(KD):
                    act.wait_ge(act_done, did.n)
                    nc.scalar.activation(squares(width)[:, k, :], src[:, k, :], ACT.Square).then_inc(act_done,
                        did.up(("square", tag, k)))
                deviation(tag, "eps2", width)
            shifted(("ctx1",), hc, hc, KD, lambda k: modv[:, k, 1:2])
            shifted(("x1",), xT, xT, KD, lambda k: modv[:, k, 0:1])

            def convolved(c):
                dst = conv_x[:, c % 2] if c < XC else (b_t[:, c - XC] if c < XC + GROUPS else c_t[:, c - XC - GROUPS])
                act.wait_ge(dve_done, when("conv", "x", c))
                act.wait_ge(act_done, did.n)
                nc.scalar.activation(dst, conv_x[:, c % 2], ACT.Silu, bias=col2("conv_b", c)).then_inc(act_done,
                    did.up(("conv_out", "x", c)))
                if c < XC + GROUPS:
                    act.wait_ge(dve_done, when("conv", "c", c))
                    act.wait_ge(act_done, did.n)
                    nc.scalar.activation(conv_c[:, c % 2], conv_c[:, c % 2], ACT.Silu, bias=col2("conv_b",
                        c)).then_inc(act_done, did.up(("conv_out", "c", c)))

            def to_tokens(c):
                for kind, n, xd, bd in (("x", TB, xtok, btok), ("c", CB, xctx, bctx)):
                    dst, o = (xd, c * P) if c < XC else (bd, (c - XC) * P)
                    act.wait_ge(pe_done, when("full", "tok", kind, c))
                    act.wait_ge(act_done, did.n)
                    nc.scalar.activation(dst[:, :, o:o + P], bank_of("tok", kind, c)[:,
                        0:n * P].rearrange("p (b m) -> p b m", m=P), ACT.Copy).then_inc(act_done, did.up(("free",
                        "tok", kind, c), ("tokens", kind, c)))

            act.wait_ge(dve_done, when("pads2"))
            for c in range(XC + 2 * GROUPS):
                for kind, pad, width in (("x", pad_x, T), ("c", pad_c, CTX)):
                    if kind == "c" and c >= XC + GROUPS:
                        continue
                    if c >= 2:
                        act.wait_ge(dve_done, when("conv", kind, c - 2))
                    act.wait_ge(pe_done, when("full", "chan", kind, c))
                    act.wait_ge(act_done, did.n)
                    nc.scalar.activation(pad[:, c % 2, 2:width + 2], bank_of("chan", kind, c)[:, 0:width],
                        ACT.Copy).then_inc(act_done, did.up(("free", "chan", kind, c), ("chan_kept", kind, c)))
                if c >= 1:
                    convolved(c - 1)
                if c >= 2 and c - 2 < XC + GROUPS:
                    to_tokens(c - 2)
            convolved(XC + 2 * GROUPS - 1)
            act.wait_ge(dve_done, when("dt_abs"))
            act.wait_ge(act_done, did.n)
            nc.scalar.activation(dt[:], dt[:], ACT.Exp, scale=-1.0).then_inc(act_done, did.up())
            act.wait_ge(act_done, did.n)
            nc.scalar.activation(dt[:], dt[:], ACT.Ln, bias=const("ones")[:, 0:1]).then_inc(act_done,
                did.up(("dt_log",)))
            act.wait_ge(act_done, did.n)
            nc.scalar.activation(row("a_log"), row("a_log"), ACT.Exp).then_inc(act_done, did.up(("a_exp",)))
            flat = lambda a: a.rearrange("p b n -> p (b n)")
            act.wait_ge(pe_done, when("full", "cs"))
            act.wait_ge(act_done, did.n)
            nc.scalar.activation(flat(ecs), bank_of("cs")[:, 0:NB * DT_W], ACT.Exp).then_inc(act_done, did.up())
            act.wait_ge(pe_done, when("full", "cs"))
            act.wait_ge(act_done, did.n)
            nc.scalar.activation(flat(cs), bank_of("cs")[:, 0:NB * DT_W], ACT.Copy).then_inc(act_done,
                did.up(("free", "cs"), ("cs_kept",)))
            act.wait_ge(pe_done, when("full", "total"))
            act.wait_ge(act_done, did.n)
            nc.scalar.activation(flat(etot), bank_of("total")[:, 0:NB * DT_W], ACT.Exp).then_inc(act_done,
                did.up(("exps2",)))
            act.wait_ge(dve_done, when("wdec_arg"))
            act.wait_ge(act_done, did.n)
            nc.scalar.activation(wdec[:], wdec[:], ACT.Exp).then_inc(act_done, did.up(("wdec_exp",)))
            for s, (d, kind, b) in enumerate(SCAN):
                if kind == "x":
                    for g in range(GROUPS):
                        if g >= 2:
                            act.wait_ge(pe_done, when("full", "yd", s, g - 2))
                        elif SCAN_BEFORE_X[s] is not None:
                            act.wait_ge(pe_done, when("full", "yd", SCAN_BEFORE_X[s], g + 2))
                        for half in range(2):
                            act.wait_ge(pe_done, when("full", "seg", s, g, half))
                            act.wait_ge(act_done, did.n)
                            nc.scalar.activation(seg[:, g % 2, half * GW:(half + 1) * GW], bank_of("seg", s, g,
                                half)[:, 0:GW], ACT.Exp).then_inc(act_done, did.up(("free", "seg", s, g, half),
                                ("seg_exp", s, g)))
            for cg in range(SSD_W // 512):
                for b in range(TB):
                    i = cg * TB + b
                    if i >= 2:
                        act.wait_ge(dve_done, when("gated", i - 2))
                    else:
                        act.wait_ge(dve_done, when("scan_done"))
                    act.wait_ge(pe_done, when("full", "z", cg, b))
                    act.wait_ge(act_done, did.n)
                    nc.scalar.activation(zs[:, i % 2, :], bank_of("z", cg, b)[:], ACT.Silu).then_inc(act_done,
                        did.up(("free", "z", cg, b), ("z_silu", i)))
            for b in range(TB):
                act.wait_ge(dve_done, when("gated", (SSD_W // 512 - 1) * TB + b))
                act.wait_ge(act_done, did.n)
                nc.scalar.activation(sq[:, 0:3, :].rearrange("p k t -> p (k t)"), ytok[:, b, :], ACT.Square,
                    accum_out=sumsq[:, b:b + 1]).then_inc(act_done, did.up())
            act.wait_ge(act_done, did.n)
            nc.scalar.activation(rs_tok[:], sumsq[:], ACT.Sqrt, bias=const("eps2"),
                scale=1.0 / SSD_W).then_inc(act_done, did.up(("tok_dev",)))
            act.wait_ge(dve_done, when("pool_pads"))
            for g in range(4):
                if g >= 2:
                    act.wait_ge(dve_done, when("pooled", g - 2))
                act.wait_ge(pe_done, when("full", "pool", g))
                act.wait_ge(act_done, did.n)
                nc.scalar.activation(pool_in[:, g % 2, :, POOL_PAD:POOL_PAD + GRID_W], bank_of("pool",
                    g)[:].rearrange("p (r t) -> p r t", t=GRID_W), ACT.Copy).then_inc(act_done, did.up(("free",
                    "pool", g), ("pool_kept", g)))
            for g in range(4):
                act.wait_ge(pe_done, when("full", "poolw", g))
                act.wait_ge(act_done, did.n)
                nc.scalar.activation(mixed[:, XC + g, :], bank_of("poolw", g)[:], ACT.Copy, scale=col2("pool_scale",
                    g)).then_inc(act_done, did.up(("free", "poolw", g), ("mixed", XC + g)))
            for c in range(XC):
                act.wait_ge(pe_done, when("full", "yt", c))
                act.wait_ge(act_done, did.n)
                nc.scalar.activation(mixed[:, c, :], bank_of("yt", c)[:], ACT.Copy, scale=col2("ssd_norm_w",
                    c)).then_inc(act_done, did.up(("free", "yt", c), ("mixed", c)))

            act.wait_ge(dve_done, when("mixer_out"))
            for k in range(KD):
                act.wait_ge(act_done, did.n)
                nc.scalar.activation(sq[:, k, :], hT[:, k, :], ACT.Square).then_inc(act_done, did.up(("square",
                    ("x2",), k)))
            deviation(("x2",), "eps2")
            shifted(("x2",), xT, xT, KD, lambda k: modv[:, 3 * KD + k, 0:1])
            for b in range(TB):
                for half in range(2):
                    act.wait_ge(pe_done, when("full", "h2t", b, half))
                    act.wait_ge(act_done, did.n)
                    nc.scalar.activation(h2_hi[:, b, half * 512:(half + 1) * 512], bank_of("h2t", b, half)[:],
                        ACT.Copy).then_inc(act_done, did.up(("h2_hi", b, half)))
            act.wait_ge(dve_done, when("logits_less_max"))
            act.wait_ge(act_done, did.n)
            nc.scalar.activation(gate, gate, ACT.Exp).then_inc(act_done, did.up(("gate_exp",)))
            n_tiles = io["wstream"].shape[0]
            by_slot = lambda b: banks[b][:].rearrange("p (k s) -> p k s", s=P)
            for half in range(2):
                act.wait_ge(pe_done, when("first_xg", half))
                act.wait_ge(act_done, did.n)
                nc.scalar.activation(xg_hi[:, 4 * half:4 * half + 4, :], by_slot(4 + half),
                    ACT.Copy).then_inc(act_done, did.up(("first_xg_hi", half)))
            act.wait_ge(dve_done, when("table"))
            with act.Fori(0, blocks_of(act)) as i:
                turn_did = Count("act", found, ("moe",))


                def round_tile(t):
                    act.wait_ge(s_tile[t % RING], i * (16 * MOE_TILES // RING) + 16 * (n_tiles // RING + t // RING + 1))
                    act.wait_ge(s_freed, i * MOE_TILES + (t + 1))
                    nc.scalar.activation(w_hi[:, t % SPLITS, :], ring[:, t % RING, :], ACT.Copy).then_inc(s_hi, 1)

                for t in range(2 * KD + SPLITS - 1):
                    round_tile(t)
                act.wait_ge(moe_dve_done, in_turn(i, "g_part"))
                nc.scalar.activation(sig, g_part, ACT.Sigmoid, scale=SWIGLU_ALPHA).then_inc(moe_act_done,
                    turn_did.up(("sig",)))
                for half in range(2):
                    act.wait_ge(moe_pe_done, in_turn(i, "xg", half))
                    nc.scalar.activation(xg_hi[:, 4 * half:4 * half + 4, :], by_slot(4 + half),
                        ACT.Copy).then_inc(moe_act_done, turn_did.up(("xg_hi", half)))
                for half in range(2):
                    act.wait_ge(moe_pe_done, in_turn(i, "act_t", half))
                    nc.scalar.activation(act_hi[:, 4 * half:4 * half + 4, :], by_slot(6 + half),
                        ACT.Copy).then_inc(moe_act_done, turn_did.up(("act_hi", half)))
                act.wait_ge(moe_pe_done, in_turn(i, "gate_t"))
                nc.scalar.activation(gate_t, banks[0][:], ACT.Copy).then_inc(moe_act_done,
                    turn_did.up(("gate_t_kept",)))
                for t in range(2 * KD + SPLITS - 1, MOE_TILES):
                    round_tile(t)
                turn_did.close()
            act.wait_ge(dve_done, when("experts_done"))
            for k in range(KD):
                act.wait_ge(act_done, did.n)
                nc.scalar.activation(sq[:, k, :], hT[:, k, :], ACT.Square).then_inc(act_done, did.up(("square",
                    ("final",), k)))
            deviation(("final",), "eps2")

        @block.vector
        def _(dve):
            did = Count("dve", found)
            norms = []


            def inverse(tag, width=T):
                out = rstd[:, len(norms) % 2, 0:width]
                norms.append(tag)
                dve.wait_ge(act_done, when("deviation", tag))
                nc.vector.reciprocal(out, out).then_inc(dve_done, did.up())
                dve.wait_ge(dve_done, did.n)
                return out

            def centre(tag, src, n):
                dve.wait_ge(pe_done, when("full", "mean", tag))
                mean = bank_of("mean", tag)
                for k in range(n):
                    dve.wait_ge(dve_done, did.n)
                    nc.vector.tensor_tensor(src[:, k, :], src[:, k, :], mean[:], ALU.subtract).then_inc(dve_done,
                        did.up(("centred", tag, k), *([("free", "mean", tag)] if k == n - 1 else [])))

            def scaled(tag, dst, src, n, gcol):
                inv = inverse(tag)
                for k in range(n):
                    dve.wait_ge(dve_done, did.n)
                    nc.vector.scalar_tensor_tensor(out=dst[:, k, :], in0=src[:, k, :], scalar=gcol(k), in1=inv,
                        op0=ALU.mult, op1=ALU.mult).then_inc(dve_done, did.up(("normed", tag, k), *([("normed_all",
                        tag)] if k == n - 1 else [])))

            def conv(dst, padded, taps, w):
                n = len(dst)
                for j in range(taps):
                    for c in range(n):
                        a, b = padded(c)[:, j:j + T], w(c, j)
                        if j == 0:
                            dve.wait_ge(dve_done, did.n)
                            nc.vector.tensor_scalar(dst[c], a, b, None, ALU.mult).then_inc(dve_done, did.up())
                        else:
                            dve.wait_ge(dve_done, did.all_but(n - 1))
                            nc.vector.scalar_tensor_tensor(out=dst[c], in0=a, scalar=b, in1=dst[c], op0=ALU.mult,
                                op1=ALU.add).then_inc(dve_done, did.up())

            nc.vector.memset(padc[:], 0.0).then_inc(dve_done, did.up())
            nc.vector.memset(pads[:], 0.0).then_inc(dve_done, did.up())
            dve.wait_ge(s_in, 16 * 5)
            q = slice(64, 96)
            ang, turns = score[q, 0, :], score[q, 1, :]
            nc.vector.tensor_copy(ang, pos_i[q, :]).then_inc(dve_done, did.up())
            dve.wait_ge(dve_done, did.n)
            dve.wait_ge(dve_done, did.n)
            nc.vector.tensor_scalar(ang, ang, const("inv_freq")[q, :], None, ALU.mult).then_inc(dve_done, did.up())
            dve.wait_ge(dve_done, did.n)
            for out, shift in ((sin_t, 0.0), (cos_t, 0.25)):
                o = out[q, :]
                dve.wait_ge(dve_done, did.n)
                nc.vector.tensor_scalar(turns, ang, 1.0 / TWO_PI, shift, ALU.mult, ALU.add).then_inc(dve_done,
                    did.up())
                dve.wait_ge(dve_done, did.n)
                dve.wait_ge(dve_done, did.n)
                nc.vector.tensor_scalar(turns, turns, ROUNDER, None, ALU.add).then_inc(dve_done, did.up())
                dve.wait_ge(dve_done, did.n)
                dve.wait_ge(dve_done, did.n)
                nc.vector.tensor_scalar(turns, turns, ROUNDER, None, ALU.subtract).then_inc(dve_done, did.up())
                dve.wait_ge(dve_done, did.n)
                dve.wait_ge(dve_done, did.n)
                nc.vector.scalar_tensor_tensor(out=o, in0=turns, scalar=-TWO_PI_PARTS[0], in1=ang, op0=ALU.mult,
                    op1=ALU.add).then_inc(dve_done, did.up())
                dve.wait_ge(dve_done, did.n)
                for part in TWO_PI_PARTS[1:]:
                    dve.wait_ge(dve_done, did.n)
                    nc.vector.scalar_tensor_tensor(out=o, in0=turns, scalar=-part, in1=o, op0=ALU.mult,
                        op1=ALU.add).then_inc(dve_done, did.up())
                    dve.wait_ge(dve_done, did.n)
                dve.wait_ge(dve_done, did.n)
                nc.vector.tensor_scalar(o, o, shift * TWO_PI, PI_BELOW, ALU.add, ALU.min).then_inc(dve_done, did.up())
                dve.wait_ge(dve_done, did.n)
                dve.wait_ge(dve_done, did.n)
                nc.vector.tensor_scalar(o, o, -PI_BELOW, None, ALU.max).then_inc(dve_done, did.up(("angles",)))
                dve.wait_ge(dve_done, did.n)
            dve.wait_ge(act_done, when("sines"))
            dve.wait_ge(dve_done, did.n)
            nc.vector.tensor_scalar(sin_t[q, :], sin_t[q, :], const("sin_sign")[q, :], None,
                ALU.mult).then_inc(dve_done, did.up())
            did.note("norm_in", ("in",))
            centre(("in",), xT, KD)
            scaled(("in",), xT, xT, KD, lambda k: col(None, "ln_in_g", k))
            for l in range(DEPTH):
                for c in range(2):
                    dve.wait_ge(act_done, when("proj", l, f"gate{c}"))
                    dve.wait_ge(dve_done, did.n)
                    nc.vector.tensor_tensor(padc[:, c, 15:T + 15], proj[:, SLOT["a0"] + c, :], proj[:,
                        SLOT["gate0"] + c, :], ALU.mult).then_inc(dve_done, did.up())
                dve.wait_ge(dve_done, did.n)
                conv([proj[:, SLOT["a0"] + c, :] for c in range(2)], lambda c: padc[:, c], CFM_TAPS,
                     lambda c, j: col(l, "cfm_w", c * CFM_TAPS + j))
                did.note("norm_in", ("cfm", l))
                dve.wait_ge(act_done, when("proj", l, "misc"))
                dve.wait_ge(dve_done, did.n)
                nc.vector.tensor_tensor(turned[q, 0, :], proj[q, SLOT["misc"], :], cos_t[q, :],
                    ALU.mult).then_inc(dve_done, did.up())
                dve.wait_ge(pe_done, when("full", "kswap", l))
                dve.wait_ge(dve_done, did.n)
                nc.vector.tensor_tensor(turned[q, 1, :], bank_of("kswap", l)[q, :], sin_t[q, :],
                    ALU.mult).then_inc(dve_done, did.up(("free", "kswap", l)))
                dve.wait_ge(dve_done, did.n)
                for h in range(HEADS):
                    dve.wait_ge(dve_done, did.n)
                    nc.vector.tensor_tensor(kc[q, h, :], turned[q, 0, :], turned[q, 1, :],
                        ALU.add).then_inc(dve_done, did.up(("keys", l)))
                for c in range(2):
                    dve.wait_ge(act_done, when("proj", l, f"h{c}"))
                    dve.wait_ge(dve_done, did.n)
                    nc.vector.tensor_tensor(pads[:, c, 1:T + 1], proj[:, SLOT["c0"] + c, :], proj[:, SLOT["h0"] + c,
                        :], ALU.mult).then_inc(dve_done, did.up())
                dve.wait_ge(dve_done, did.n)
                conv([y[:, c, :] for c in range(2)], lambda c: pads[:, c], 3, lambda c, j: col(l, "sc_w", c * 3 + j))
                dve.wait_ge(dve_done, did.n)
                for c in range(2):
                    dve.wait_ge(dve_done, did.n)
                    nc.vector.tensor_tensor(y[:, c, :], y[:, c, :], proj[:, SLOT["b0"] + c, :],
                        ALU.mult).then_inc(dve_done, did.up(("ya", l)))
                ckv, cq = proj[:, SLOT["ckv"]:SLOT["ckv"] + 1, :], proj[:, SLOT["cq0"]:SLOT["cq0"] + 2, :]
                scaled(("kv", l), ckv, ckv, 1, lambda k: col(l, "mla_kv_g"))
                scaled(("q", l), cq, cq, 2, lambda k: col(l, "mla_q_g", k))
                for h in range(HEADS):
                    dve.wait_ge(pe_done, when("full", "qh", l, h))
                    src = bank_of("qh", l, h)
                    dve.wait_ge(dve_done, did.n)
                    nc.vector.tensor_tensor(turned[q, 0, :], src[q, :], cos_t[q, :], ALU.mult).then_inc(dve_done,
                        did.up())
                    nc.vector.tensor_copy(qc[0:NOPE, h, :], src[0:NOPE, :]).then_inc(dve_done, did.up(("free", "qh",
                        l, h)))
                    dve.wait_ge(pe_done, when("full", "qswap", l, h))
                    dve.wait_ge(dve_done, did.n)
                    nc.vector.tensor_tensor(turned[q, 1, :], bank_of("qswap", l, h)[q, :], sin_t[q, :],
                        ALU.mult).then_inc(dve_done, did.up(("free", "qswap", l, h)))
                    dve.wait_ge(dve_done, did.n)
                    dve.wait_ge(dve_done, did.n)
                    nc.vector.tensor_tensor(qc[q, h, :], turned[q, 0, :], turned[q, 1, :],
                        ALU.add).then_inc(dve_done, did.up(("query", l, h)))
                for d in range(2):
                    dve.wait_ge(pe_done, when("full", "la", l, d))
                    dve.wait_ge(dve_done, did.n)
                    nc.vector.tensor_scalar(z_la[:, d, :], bank_of("la", l, d)[:], col(l, "gla_b", d), None,
                        ALU.add).then_inc(dve_done, did.up(("free", "la", l, d)))
                for i in range(HEADS * TB):
                    dve.wait_ge(act_done, when("score_kept", l, i))
                    nc.vector.tensor_reduce(negmax[:, i:i + 1], score[:, i % 2, :], AX, ALU.max,
                        negate=True).then_inc(dve_done, did.up(("negmax", l, i)))
                    dve.wait_ge(act_done, when("exps", l, i))
                    nc.vector.reciprocal(rsum[:, i:i + 1], rsum[:, i:i + 1]).then_inc(dve_done, did.up())
                    dve.wait_ge(dve_done, did.n)
                    dve.wait_ge(dve_done, did.n)
                    nc.vector.tensor_scalar(probs[:, i % 2, :], probs[:, i % 2, :], rsum[:, i:i + 1], None,
                        ALU.mult).then_inc(dve_done, did.up(("probs", l, i)))
                dve.wait_ge(act_done, when("yc", l, HEADS - 1))
                nc.vector.memset(qdiag, 0.0).then_inc(dve_done, did.up())
                nc.vector.memset(kdec, 0.0).then_inc(dve_done, did.up())
                dve.wait_ge(dve_done, did.n)
                for d in range(2):
                    dve.wait_ge(dve_done, did.n)
                    nc.vector.scalar_tensor_tensor(out=e_la[:, d, :], in0=z_la[:, d, :], scalar=-1.0, in1=z_la[:, d,
                        :], op0=ALU.mult, op1=ALU.max).then_inc(dve_done, did.up(("la_abs", l, d)))
                for d in range(2):
                    dve.wait_ge(act_done, when("la_log", l, d))
                    dve.wait_ge(dve_done, did.n)
                    nc.vector.scalar_tensor_tensor(out=z_la[:, d, :], in0=z_la[:, d, :], scalar=0.0, in1=e_la[:, d,
                        :], op0=ALU.min, op1=ALU.subtract).then_inc(dve_done, did.up())
                dve.wait_ge(dve_done, did.n)
                for d in range(2):
                    dve.wait_ge(dve_done, did.n)
                    nc.vector.tensor_scalar(z_la[:, d, :], z_la[:, d, :], (1.0, -1.0)[d] / GLA_TAU, None,
                        ALU.mult).then_inc(dve_done, did.up())
                nc.vector.memset(cpos[:, 1, 0:1], 0.0).then_inc(dve_done, did.up())
                dve.wait_ge(dve_done, did.n)
                one = const("ones")[:, 0:1]
                nc.vector.tensor_tensor_scan(cpos[:, 0, :], one.to_broadcast([P, T]), z_la[:, 0, :], 0.0, ALU.mult,
                    ALU.add).then_inc(dve_done, did.up())
                nc.vector.tensor_tensor_scan(cpos[:, 1, 1:T], one.to_broadcast([P, T - 1]), z_la[:, 1, 0:T - 1], 0.0,
                    ALU.mult, ALU.add).then_inc(dve_done, did.up())
                dve.wait_ge(dve_done, did.n)
                for d in range(2):
                    dve.wait_ge(dve_done, did.n)
                    nc.vector.tensor_scalar(cneg[:, d, :], cpos[:, d, :], -1.0, None, ALU.mult).then_inc(dve_done,
                        did.up())
                    pos = cpos[:, d, :].rearrange("p (n s) -> p n s", s=SUB)
                    anchor = pos[:, :, (0, SUB - 1)[d]:(1, SUB)[d]].to_broadcast([P, T // SUB, SUB])
                    dve.wait_ge(dve_done, did.n)
                    nc.vector.tensor_tensor(z_la[:, d, :].rearrange("p (n s) -> p n s", s=SUB), pos, anchor,
                        ALU.subtract).then_inc(dve_done, did.up(("qdiag_arg", l)))
                for d in range(2):
                    dve.wait_ge(act_done, when("qdiag_exp", l, d))
                    for h in range(HEADS):
                        hp = slice(DK * h, DK * (h + 1))
                        out = qdiag[hp, d].rearrange("p j (i h t) -> p (j i) h t", h=HEADS, t=SUB)[:, :, h, :]
                        dve.wait_ge(dve_done, did.n)
                        nc.vector.tensor_tensor(out, z_la[hp, d, :].rearrange("p (n s) -> p n s", s=SUB), proj[hp,
                            SLOT["q"], :].rearrange("p (n s) -> p n s", s=SUB), ALU.mult).then_inc(dve_done,
                            did.up())
                for j in range(TB):
                    kj = proj[:, SLOT["k"], j * P:(j + 1) * P]
                    for d in range(2):
                        dve.wait_ge(act_done, when("kdec_exp", l, j, d))
                        dve.wait_ge(dve_done, did.n)
                        nc.vector.scalar_tensor_tensor(out=kdec[:, d], in0=kdec[:, d], scalar=BOUND,
                            in1=kj.unsqueeze(1).to_broadcast([P, NSUB, P]), op0=ALU.min,
                            op1=ALU.mult).then_inc(dve_done, did.up(("kdec", l, j, d)))
                    for d in range(2):
                        if 0 < (TB - 1 - j, j)[d]:
                            t0, t1 = (((j + 1) * P, T), (0, j * P))[d]
                            dve.wait_ge(act_done, when("qhat_exp", l, j, d))
                            dve.wait_ge(dve_done, did.n)
                            nc.vector.tensor_tensor(khat[:, d, j % 2, :], khat[:, d, j % 2, :], kj,
                                ALU.mult).then_inc(dve_done, did.up())
                            dve.wait_ge(dve_done, did.n)
                            nc.vector.tensor_tensor(qhat[:, d, j % 2, t0:t1], qhat[:, d, j % 2, t0:t1], proj[:,
                                SLOT["q"], t0:t1], ALU.mult).then_inc(dve_done, did.up(("qhat", l, j, d)))
                    for d, mask in enumerate((const("upto"), const("after"))):
                        dve.wait_ge(pe_done, when("full", "gdiag", l, j, d))
                        src = bank_of("gdiag", l, j, d)[:].rearrange("p (i h t) -> p h i t", h=HEADS, t=SUB)
                        m = mask.rearrange("p (i t) -> p i t", t=SUB).unsqueeze(1).to_broadcast([P, HEADS, NSUB, SUB])
                        dve.wait_ge(dve_done, did.n)
                        nc.vector.tensor_tensor(dtmp[:, d].rearrange("p (h i t) -> p h i t", h=HEADS, t=SUB), src, m,
                            ALU.mult).then_inc(dve_done, did.up(("free", "gdiag", l, j, d)))
                    dve.wait_ge(dve_done, did.n)
                    for g, am in enumerate((amat01, amat23)):
                        dve.wait_ge(dve_done, did.n)
                        nc.vector.tensor_tensor(am[:, :, j, j * P:(j + 1) * P], dtmp[:, 0,
                            g * MIX:(g + 1) * MIX].rearrange("p (h t) -> p h t", h=2), dtmp[:, 1,
                            g * MIX:(g + 1) * MIX].rearrange("p (h t) -> p h t", h=2), ALU.add).then_inc(dve_done,
                            did.up())
                    dve.wait_ge(dve_done, did.n)
                dve.wait_ge(act_done, when("amat_off", l))
                nc.vector.memset(negmax[:, 0:1], 0.0).then_inc(dve_done, did.up(("amat", l)))
                for c in range(2):
                    o = proj[:, SLOT["b0"] + c, :]
                    dve.wait_ge(dve_done, did.n)
                    nc.vector.scalar_tensor_tensor(out=o, in0=o, scalar=col(l, "gla_head_g", c), in1=inverse(("gla",
                        l, c)), op0=ALU.mult, op1=ALU.mult).then_inc(dve_done, did.up(("normed_all", ("gla", l, c))))
                    dve.wait_ge(dve_done, did.n)
                    dve.wait_ge(dve_done, did.n)
                    nc.vector.tensor_tensor(y[:, 2 + c, :], o, proj[:, SLOT["gg0"] + c, :],
                        ALU.mult).then_inc(dve_done, did.up(("yb_gated", l)))
                centre(("cfm", l), proj, 2)
                scaled(("cfm", l), proj, proj, 2, lambda k: col(l, "cfm_g", k))
                dve.wait_ge(act_done, when("norm_out", ("cfm", l), 1))
                for b in range(4):
                    scaled(("branch", l, b), yn[:, 2 * b:2 * b + 2, :], y[:, 2 * b:2 * b + 2, :], 2,
                           lambda k: col(l, "branch_g", 2 * b + k))
                for m in range(KD):
                    dve.wait_ge(pe_done, when("full", "mix", l, m))
                    dve.wait_ge(dve_done, did.n)
                    nc.vector.scalar_tensor_tensor(out=xT[:, m, :], in0=hT[:, m, :], scalar=ALPHA, in1=bank_of("mix",
                        l, m)[:], op0=ALU.mult, op1=ALU.add).then_inc(dve_done, did.up(("free", "mix", l, m),
                        ("norm_in", ("ln1", l))))
                dve.wait_ge(dve_done, did.n)
                centre(("ln1", l), xT, KD)
                scaled(("ln1", l), xT, xT, KD, lambda k: col(l, "ln1_g", k))
                dve.wait_ge(pe_done, when("full", "mix", l, KD - 1))
                nc.vector.memset(ubuf[:, :, 0:1], 0.0).then_inc(dve_done, did.up())
                nc.vector.memset(ubuf[:, :, T + 1:T + 2], 0.0).then_inc(dve_done, did.up(("pads_ff", l)))
                for c in range(KF):
                    for v in range(2):
                        dve.wait_ge(act_done, when("up_kept", l, c, v))
                        i = 2 * c + v
                        if v == 0 and c >= 2:
                            dve.wait_ge(act_done, when("silu_ff", l, c - 2))
                        w = lambda j: col(l, "ffn_w", (v * KF + c) * FFN_TAPS + j)
                        dve.wait_ge(dve_done, did.n)
                        nc.vector.tensor_scalar(cbuf[:, i % 4, :], ubuf[:, i % 4, 0:T], w(0), None,
                            ALU.mult).then_inc(dve_done, did.up())
                        dve.wait_ge(dve_done, did.n)
                        dve.wait_ge(dve_done, did.n)
                        nc.vector.scalar_tensor_tensor(out=cbuf[:, i % 4, :], in0=ubuf[:, i % 4, 1:T + 1],
                            scalar=w(1), in1=cbuf[:, i % 4, :], op0=ALU.mult, op1=ALU.add).then_inc(dve_done,
                            did.up())
                        dve.wait_ge(dve_done, did.n)
                        dve.wait_ge(dve_done, did.n)
                        nc.vector.scalar_tensor_tensor(out=cbuf[:, i % 4, :], in0=ubuf[:, i % 4, 2:T + 2],
                            scalar=w(2), in1=cbuf[:, i % 4, :], op0=ALU.mult, op1=ALU.add).then_inc(dve_done,
                            did.up(("conv_ff", l, c, v)))
                    dve.wait_ge(dve_done, did.n)
                    dve.wait_ge(act_done, when("silu_ff", l, c))
                    dve.wait_ge(dve_done, did.n)
                    nc.vector.tensor_tensor(act_ff[:, c, :], gbuf[:, c % 2, :], cbuf[:, (2 * c + 1) % 4, :],
                        ALU.mult).then_inc(dve_done, did.up(("act_ff", l, c)))
                for m in range(KD):
                    dve.wait_ge(pe_done, when("full", "down", l, m))
                    dve.wait_ge(dve_done, did.n)
                    nc.vector.scalar_tensor_tensor(out=xT[:, m, :], in0=hT[:, m, :], scalar=ALPHA,
                        in1=bank_of("down", l, m)[:], op0=ALU.mult, op1=ALU.add).then_inc(dve_done, did.up(("free",
                        "down", l, m), ("norm_in", ("ln2", l))))
                dve.wait_ge(dve_done, did.n)
                centre(("ln2", l), xT, KD)
                scaled(("ln2", l), xT, xT, KD, lambda k: col(l, "ln2_g", k))
            dve.wait_ge(pe_done, when("full", "mod"))
            dve.wait_ge(dve_done, did.n)
            nc.vector.tensor_tensor(modv[:], bank_of("mod")[:, 0:12 * KD].rearrange("p (m c) -> p m c", c=2),
                col2("b_mod", 0, 6 * KD).unsqueeze(2).to_broadcast([P, 6 * KD, 2]), ALU.add).then_inc(dve_done,
                did.up(("free", "mod")))
            for i, (section, which, name) in enumerate(((1, 1, "norm1_w"), (1, 0, "norm1_w"), (4, 0, "norm2_w"))):
                dve.wait_ge(dve_done, did.n)
                nc.vector.scalar_tensor_tensor(out=gains[:, i, :], in0=modv[:, section * KD:(section + 1) * KD,
                    which], scalar=1.0, in1=col2(name, 0, KD), op0=ALU.add, op1=ALU.mult).then_inc(dve_done,
                    did.up())

            def rms_scaled(tag, dst, src, gain, width=T):
                inv = inverse(tag, width)
                for k in range(KD):
                    dve.wait_ge(dve_done, did.n)
                    nc.vector.scalar_tensor_tensor(out=dst[:, k, :], in0=src[:, k, :], scalar=gain(k), in1=inv,
                        op0=ALU.mult, op1=ALU.mult).then_inc(dve_done, did.up(("normed", tag, k), *([("normed_all",
                        tag)] if k == KD - 1 else [])))

            nc.vector.memset(padc[:], 0.0).then_inc(dve_done, did.up())
            nc.vector.memset(pads[:], 0.0).then_inc(dve_done, did.up(("pads2",)))
            rms_scaled(("ctx1",), hc, hc, lambda k: gains[:, 0, k:k + 1], CTX)
            rms_scaled(("x1",), xT, hT, lambda k: gains[:, 1, k:k + 1])
            flat = lambda a: a.rearrange("p b n -> p (b n)")
            spread = lambda name: row(name).unsqueeze(1).to_broadcast([P, NB, DT_W])
            dve.wait_ge(pe_done, when("full", "dt"))
            dve.wait_ge(dve_done, did.n)
            nc.vector.tensor_tensor(dt_raw[:], bank_of("dt")[:, 0:NB * DT_W].rearrange("p (b n) -> p b n", n=DT_W),
                spread("dt_bias"), ALU.add).then_inc(dve_done, did.up(("free", "dt")))
            dve.wait_ge(dve_done, did.n)
            nc.vector.scalar_tensor_tensor(out=flat(dt), in0=flat(dt_raw), scalar=-1.0, in1=flat(dt_raw),
                op0=ALU.mult, op1=ALU.max).then_inc(dve_done, did.up(("dt_abs",)))

            def convolve(c):
                kinds = [("x", pad_x, conv_x, T), ("c", pad_c, conv_c, CTX)][:2 if c < XC + GROUPS else 1]
                for kind, pad, dst, width in kinds:
                    dve.wait_ge(act_done, when("chan_kept", kind, c))
                if c >= 2:
                    if c - 2 < XC + GROUPS:
                        dve.wait_ge(pe_done, when("full", "tok", "x", c - 2))
                        dve.wait_ge(pe_done, when("full", "tok", "c", c - 2))
                    dve.wait_ge(act_done, when("conv_out", "x", c - 2))
                dve.wait_ge(dve_done, did.n)
                for j in range(SSD_TAPS):
                    for kind, pad, dst, width in kinds:
                        out, a, w = dst[:, c % 2], pad[:, c % 2, j:j + width], col2("conv_w", c * SSD_TAPS + j)
                        names = [("conv", kind, c)] if j == SSD_TAPS - 1 else []
                        dve.wait_ge(dve_done, did.all_but(len(kinds) - 1))
                        if j == 0:
                            nc.vector.tensor_scalar(out, a, w, None, ALU.mult).then_inc(dve_done, did.up(*names))
                        else:
                            nc.vector.scalar_tensor_tensor(out=out, in0=a, scalar=w, in1=out, op0=ALU.mult,
                                op1=ALU.add).then_inc(dve_done, did.up(*names))

            for c in range(XC + 2 * GROUPS):
                convolve(c)
            dve.wait_ge(act_done, when("dt_log"))
            dve.wait_ge(dve_done, did.n)
            nc.vector.scalar_tensor_tensor(out=flat(dt), in0=flat(dt_raw), scalar=0.0, in1=flat(dt), op0=ALU.max,
                op1=ALU.add).then_inc(dve_done, did.up())
            dve.wait_ge(act_done, when("a_exp"))
            dve.wait_ge(dve_done, did.n)
            nc.vector.tensor_tensor(la[:], dt[:], spread("a_log"), ALU.mult).then_inc(dve_done, did.up())
            dve.wait_ge(dve_done, did.n)
            nc.vector.tensor_scalar(la[:], la[:], -1.0, None, ALU.mult).then_inc(dve_done, did.up(("la",)))
            dve.wait_ge(act_done, when("cs_kept"))
            dve.wait_ge(act_done, when("exps2"))
            dve.wait_ge(pe_done, when("full", "total"))
            dve.wait_ge(dve_done, did.n)
            nc.vector.tensor_tensor(flat(wdec), bank_of("total")[:, 0:NB * DT_W], flat(cs),
                ALU.subtract).then_inc(dve_done, did.up(("wdec_arg",)))
            dve.wait_ge(act_done, when("wdec_exp"))
            dve.wait_ge(dve_done, did.n)
            nc.vector.tensor_tensor(wdec[:], wdec[:], dt[:], ALU.mult).then_inc(dve_done, did.up(("free", "total")))
            by_head = lambda a: a.rearrange("p (h c) -> p h c", c=HEAD_W)

            def per_head(a, b, d, n=SSD_HEADS, at=0):
                return a[:, b, d * SSD_HEADS + at:d * SSD_HEADS + at + n].unsqueeze(2).to_broadcast([P, n, HEAD_W])

            dve.wait_ge(act_done, when("tokens", "c", XC + GROUPS - 1))
            for s, (d, kind, b) in enumerate(SCAN):
                blk = b if kind == "x" else TB + b
                xsrc = (xtok if kind == "x" else xctx)[:, b, :]
                hs = slice(d * SSD_HEADS, (d + 1) * SSD_HEADS)
                if s == 2 * CB:
                    dve.wait_ge(pe_done, when("full", "st", s - 1, GROUPS - 1))
                    for t in range(TB):
                        dve.wait_ge(dve_done, did.n)
                        nc.vector.tensor_tensor(by_head(ytok[:, t, :]), by_head(xtok[:, t, :]),
                            row("d_skip").unsqueeze(2).to_broadcast([P, SSD_HEADS, HEAD_W]),
                            ALU.mult).then_inc(dve_done, did.up())
                if s > 0:
                    dve.wait_ge(pe_done, when("full", "st", s - 1, GROUPS - 1))
                dve.wait_ge(dve_done, did.n)
                nc.vector.tensor_tensor(by_head(xw), by_head(xsrc), per_head(wdec, blk, d),
                    ALU.mult).then_inc(dve_done, did.up(("xw", s)))
                if kind == "x":
                    dve.wait_ge(dve_done, did.n)
                    nc.vector.tensor_tensor(by_head(xs), by_head(xsrc), per_head(dt, blk, d),
                        ALU.mult).then_inc(dve_done, did.up(("xs", s)))
                    mask = const(("upto", "from")[d])
                    dve.wait_ge(pe_done, when("full", "cb", s))
                    dve.wait_ge(dve_done, did.n)
                    nc.vector.tensor_tensor(cbm.rearrange("p (g t) -> p g t", t=P), bank_of("cb",
                        s)[:].rearrange("p (g t) -> p g t", t=P), mask.unsqueeze(1).to_broadcast([P, GROUPS, P]),
                        ALU.mult).then_inc(dve_done, did.up(("free", "cb", s)))

                    def seg_arg(g):
                        if g >= 2:
                            dve.wait_ge(pe_done, when("full", "seg", s, g - 2, 1))
                        a = d * SSD_HEADS + g * HPG
                        dve.wait_ge(dve_done, did.n)
                        nc.vector.tensor_tensor(seg_in[:, g % 2, :].rearrange("p (h t) -> p h t", t=P), la[:, blk,
                            a:a + HPG].unsqueeze(2).to_broadcast([P, HPG, P]), mask.unsqueeze(1).to_broadcast([P,
                            HPG, P]), ALU.mult).then_inc(dve_done, did.up(("seg_in", s, g)))

                    def decayed(g):
                        dve.wait_ge(act_done, when("seg_exp", s, g))
                        v = seg[:, g % 2, :].rearrange("p (h t) -> p h t", t=P)
                        dve.wait_ge(dve_done, did.n)
                        nc.vector.tensor_tensor(v, v, cbm[:, g * P:(g + 1) * P].unsqueeze(1).to_broadcast([P, HPG,
                            P]), ALU.mult).then_inc(dve_done, did.up(("amat2", s, g)))

                    def add_within(g):
                        yg = ytok[:, b, g * GW:(g + 1) * GW]
                        dve.wait_ge(pe_done, when("full", "yd", s, g))
                        dve.wait_ge(dve_done, did.n)
                        nc.vector.tensor_tensor(yg, yg, bank_of("yd", s, g)[:, 0:GW], ALU.add).then_inc(dve_done,
                            did.up(("free", "yd", s, g)))

                    seg_arg(0)
                    seg_arg(1)
                    decayed(0)
                    for g in range(GROUPS):
                        yg = ytok[:, b, g * GW:(g + 1) * GW]
                        dve.wait_ge(pe_done, when("full", "yoff", s, g))
                        dve.wait_ge(dve_done, did.n)
                        nc.vector.tensor_tensor(by_head(yoffs[:, g % 2, :]), by_head(bank_of("yoff", s, g)[:, 0:GW]),
                            per_head(ecs, blk, d, HPG, g * HPG), ALU.mult).then_inc(dve_done, did.up(("free", "yoff",
                            s, g)))
                        dve.wait_ge(dve_done, did.n)
                        nc.vector.tensor_tensor(yg, yg, yoffs[:, g % 2, :], ALU.add).then_inc(dve_done, did.up())
                    seg_arg(2)
                    decayed(1)
                    add_within(0)
                    seg_arg(3)
                    decayed(2)
                    add_within(1)
                    decayed(3)
                    add_within(2)
                    add_within(3)
                first = s < 2
                if not first:
                    dve.wait_ge(dve_done, did.n)
                    nc.vector.tensor_tensor(by_head(states[:, d, :]), by_head(states[:, d, :]), per_head(etot, blk,
                        d), ALU.mult).then_inc(dve_done, did.up())
                for g in range(GROUPS):
                    st = states[:, d, g * GW:(g + 1) * GW]
                    dve.wait_ge(pe_done, when("full", "st", s, g))
                    src = bank_of("st", s, g)[:, 0:GW]
                    if first:
                        dve.wait_ge(dve_done, did.n)
                        nc.vector.tensor_copy(st, src).then_inc(dve_done, did.up(("free", "st", s, g), ("state", s)))
                    else:
                        dve.wait_ge(dve_done, did.n)
                        nc.vector.tensor_tensor(st, st, src, ALU.add).then_inc(dve_done, did.up(("free", "st", s, g),
                            ("state", s)))
            did.note("scan_done")
            dve.wait_ge(pe_done, when("full", "st", len(SCAN) - 1, GROUPS - 1))
            nc.vector.memset(pool_in, 0.0).then_inc(dve_done, did.up(("pool_pads",)))
            for cg in range(SSD_W // 512):
                for b in range(TB):
                    i = cg * TB + b
                    dve.wait_ge(act_done, when("z_silu", i))
                    v = ytok[:, b, cg * 512:(cg + 1) * 512]
                    dve.wait_ge(dve_done, did.n)
                    nc.vector.tensor_tensor(v, v, zs[:, i % 2, :], ALU.mult).then_inc(dve_done, did.up(("gated", i)))
            dve.wait_ge(act_done, when("tok_dev"))
            nc.vector.reciprocal(rs_tok[:], rs_tok[:]).then_inc(dve_done, did.up())
            for b in range(TB):
                dve.wait_ge(dve_done, did.n)
                nc.vector.tensor_scalar(ytok[:, b, :], ytok[:, b, :], rs_tok[:, b:b + 1], None,
                    ALU.mult).then_inc(dve_done, did.up(("ynormed", b)))
            for g, window in enumerate(POOL_WINDOWS):
                dve.wait_ge(act_done, when("pool_kept", g))
                if g >= 2:
                    dve.wait_ge(pe_done, when("full", "poolw", g - 2))
                u = pool_in[:, g % 2]
                reach = [window // 2 - 1]
                lo, hi = POOL_PAD - window // 2 + 1, POOL_PAD + GRID_W + window // 2 - 1
                dve.wait_ge(dve_done, did.n)
                nc.vector.tensor_tensor(pool_s[:, 0, :, lo:hi], u[:, :, lo - 1:hi - 1], u[:, :, lo:hi],
                    ALU.add).then_inc(dve_done, did.up())
                half, cur = 1, 0
                while 2 * half < window:
                    lo, hi = lo + half, hi - half
                    dve.wait_ge(dve_done, did.n)
                    nc.vector.tensor_tensor(pool_s[:, 1 - cur, :, lo:hi], pool_s[:, cur, :, lo - half:hi - half],
                        pool_s[:, cur, :, lo + half:hi + half], ALU.add).then_inc(dve_done, did.up())
                    half, cur = 2 * half, 1 - cur
                share = const("pool_share")[:, g * GRID_W:(g + 1) * GRID_W].unsqueeze(1).to_broadcast([P, GRID_ROWS, GRID_W])
                inner = slice(POOL_PAD, POOL_PAD + GRID_W)
                dve.wait_ge(dve_done, did.n)
                nc.vector.tensor_tensor(pool_s[:, 1 - cur, :, inner], pool_s[:, cur, :, inner], share,
                    ALU.mult).then_inc(dve_done, did.up())
                dve.wait_ge(dve_done, did.n)
                nc.vector.tensor_tensor(pooled[:, g % 2, :].rearrange("p (r t) -> p r t", t=GRID_W), pool_s[:,
                    1 - cur, :, inner], u[:, :, inner], ALU.subtract).then_inc(dve_done, did.up(("pooled", g)))
            for m in range(KD):
                dve.wait_ge(pe_done, when("full", "out2", m))
                dve.wait_ge(dve_done, did.n)
                nc.vector.scalar_tensor_tensor(out=hT[:, m, :], in0=bank_of("out2", m)[:], scalar=modv[:, 2 * KD + m,
                    0:1], in1=hT[:, m, :], op0=ALU.mult, op1=ALU.add).then_inc(dve_done, did.up(("free", "out2", m),
                    ("mixer_out",)))
            rms_scaled(("x2",), xT, hT, lambda k: gains[:, 2, k:k + 1])
            dve.wait_ge(pe_done, when("full", "out2", KD - 1))
            dve.wait_ge(dve_done, did.n)
            nc.vector.memset(logits[:, :, EXPERTS:], NO_LOGIT).then_inc(dve_done, did.up())
            nc.vector.memset(sought[:, :, TOP_K:], NO_LOGIT).then_inc(dve_done, did.up())
            dve.wait_ge(pe_done, when("full", "router"))
            dve.wait_ge(dve_done, did.n)
            nc.vector.tensor_tensor(logits[:, :, 0:EXPERTS], bank_of("router")[:,
                0:TB * EXPERTS].rearrange("p (b e) -> p b e", e=EXPERTS),
                row("router_b").unsqueeze(1).to_broadcast([P, TB, EXPERTS]), ALU.add).then_inc(dve_done,
                did.up(("free", "router")))
            for b in range(TB):
                dve.wait_ge(dve_done, did.n)
                nc.vector.max(top8[:, b, :], logits[:, b, 0:EXPERTS]).then_inc(dve_done, did.up())
                dve.wait_ge(dve_done, did.n)
                nc.vector.tensor_copy(sought[:, b, 0:TOP_K], top8[:, b, 0:TOP_K]).then_inc(dve_done, did.up())
                dve.wait_ge(dve_done, did.n)
                nc.vector.tensor_scalar(gate[:, b, :], logits[:, b, 0:EXPERTS], top8[:, b, 0:1], None,
                    ALU.subtract).then_inc(dve_done, did.up(("logits_less_max",)))
                dve.wait_ge(dve_done, did.n)
                nc.vector.match_replace(marked[:, b, :], sought[:, b, :], logits[:, b, :], PICKED).then_inc(dve_done,
                    did.up())
            dve.wait_ge(dve_done, did.n)
            nc.vector.tensor_scalar(chosen, marked[:, :, 0:EXPERTS], PICKED, None, ALU.is_equal).then_inc(dve_done,
                did.up(("chosen",)))
            for b in range(TB):
                for half in range(2):
                    c = slice(half * 512, (half + 1) * 512)
                    dve.wait_ge(act_done, when("h2_hi", b, half))
                    dve.wait_ge(pe_done, when("full", "h2t", b, half))
                    dve.wait_ge(dve_done, did.n)
                    nc.vector.tensor_tensor(h2_lo[:, b, c], bank_of("h2t", b, half)[:], h2_hi[:, b, c].bitcast(F32),
                        ALU.subtract).then_inc(dve_done, did.up(("free", "h2t", b, half)))
            dve.wait_ge(act_done, when("gate_exp"))
            dve.wait_ge(dve_done, did.n)
            nc.vector.tensor_tensor(gate, gate, chosen, ALU.mult).then_inc(dve_done, did.up())
            dve.wait_ge(dve_done, did.n)
            nc.vector.tensor_reduce(gate_sum, gate, AX, ALU.add).then_inc(dve_done, did.up())
            dve.wait_ge(dve_done, did.n)
            nc.vector.reciprocal(gate_sum, gate_sum).then_inc(dve_done, did.up())
            dve.wait_ge(dve_done, did.n)
            nc.vector.tensor_tensor(gate, gate, gate_sum.unsqueeze(2).to_broadcast([P, TB, EXPERTS]),
                ALU.mult).then_inc(dve_done, did.up())
            dve.wait_ge(pe_done, when("full", "rank"))
            src = bank_of("rank")
            dve.wait_ge(dve_done, did.n)
            nc.vector.scalar_tensor_tensor(out=rank, in0=src[:, 0:TB * EXPERTS].rearrange("p (b e) -> p b e",
                e=EXPERTS), scalar=1.0, in1=chosen, op0=ALU.add, op1=ALU.mult).then_inc(dve_done, did.up())
            dve.wait_ge(dve_done, did.n)
            nc.vector.tensor_scalar(rank, rank, -1.0, None, ALU.add).then_inc(dve_done, did.up())
            count = src[:, TB * EXPERTS:(TB + 1) * EXPERTS]
            dve.wait_ge(dve_done, did.n)
            nc.vector.tensor_scalar(n_blk, count, 0.5, None, ALU.is_gt).then_inc(dve_done, did.up())
            for j in range(1, TB):
                dve.wait_ge(dve_done, did.n)
                nc.vector.tensor_scalar(above, count, j * P + 0.5, None, ALU.is_gt).then_inc(dve_done,
                    did.up(("free", "rank")))
                dve.wait_ge(dve_done, did.n)
                nc.vector.tensor_tensor(n_blk, n_blk, above, ALU.add).then_inc(dve_done, did.up())
            dve.wait_ge(dve_done, did.n)
            one = const("ones")[:, 0:1]
            nc.vector.tensor_tensor_scan(blk_end, one.to_broadcast([P, EXPERTS]), n_blk, 0.0, ALU.mult,
                ALU.add).then_inc(dve_done, did.up())
            dve.wait_ge(s_iota, 16)
            r = slice(0, 1)
            number = iota[r, 0:MAX_BLOCKS + 1]
            dve.wait_ge(dve_done, did.n)
            nc.vector.tensor_tensor(of_block[r], blk_end[r].unsqueeze(1).to_broadcast([1, MAX_BLOCKS + 1, EXPERTS]),
                number.unsqueeze(2).to_broadcast([1, MAX_BLOCKS + 1, EXPERTS]), ALU.is_le).then_inc(dve_done,
                did.up())
            dve.wait_ge(dve_done, did.n)
            nc.vector.tensor_reduce(table_f[r, 0, :], of_block[r], AX, ALU.add).then_inc(dve_done, did.up())
            dve.wait_ge(dve_done, did.n)
            nc.vector.tensor_tensor(of_block[r], of_block[r], n_blk[r].unsqueeze(1).to_broadcast([1, MAX_BLOCKS + 1,
                EXPERTS]), ALU.mult).then_inc(dve_done, did.up())
            dve.wait_ge(dve_done, did.n)
            nc.vector.tensor_reduce(table_f[r, 1, :], of_block[r], AX, ALU.add).then_inc(dve_done, did.up())
            dve.wait_ge(dve_done, did.n)
            nc.vector.tensor_tensor(table_f[r, 1, :], number, table_f[r, 1, :], ALU.subtract).then_inc(dve_done,
                did.up())
            dve.wait_ge(dve_done, did.n)
            nc.vector.tensor_scalar(table_f[r, 0, :], table_f[r, 0, :], EXPERTS - 1.0, None,
                ALU.min).then_inc(dve_done, did.up())
            dve.wait_ge(dve_done, did.n)
            nc.vector.tensor_scalar(table_f[r, 1, :], table_f[r, 1, :], TB - 1.0, None, ALU.min).then_inc(dve_done,
                did.up())
            nc.vector.tensor_copy(table_f[r, 2, :], blk_end[r, EXPERTS - 1:EXPERTS].to_broadcast([1,
                MAX_BLOCKS + 1])).then_inc(dve_done, did.up())
            dve.wait_ge(dve_done, did.n)
            for primed, key in ((moe_pe_done, "pe"), (moe_act_done, "act"), (moe_dve_done, "dve"),
                                (moe_pool_done, "pool")):
                nc.vector.memset(above[:, 0:1], 0.0).then_inc(primed, per_turn(key))
                dve.wait_ge(primed, per_turn(key))
            nc.vector.tensor_copy(table[r], table_f[r]).then_inc(dve_done, did.up(("table",)))
            dve.wait_ge(dve_done, did.n)
            e = dve.value_load(table[0:1, 0, 0:1], min_val=0, max_val=EXPERTS - 1)
            for b in range(TB):
                nc.vector.tensor_scalar(pick[:, b, :], iota[:, 0:P], rank[:, b, bass.ds(e, 1)], None,
                    ALU.is_equal).then_inc(dve_done, did.up(("first_pick",)))
            by_slot = lambda b: banks[b][:].rearrange("p (k s) -> p k s", s=P)
            nc.vector.memset(y_slot, 0.0).then_inc(dve_done, did.up())
            nc.vector.memset(gate_t, 0.0).then_inc(dve_done, did.up())
            for half in range(2):
                c = slice(4 * half, 4 * half + 4)
                dve.wait_ge(act_done, when("first_xg_hi", half))
                dve.wait_ge(dve_done, did.n)
                nc.vector.tensor_tensor(xg_lo[:, c, :], by_slot(4 + half), xg_hi[:, c, :].bitcast(F32),
                    ALU.subtract).then_inc(dve_done, did.up(("first_xg_kept",)))
            nc.vector.memset(above[:, 1:2], 0.0).then_inc(s_freed, SPLITS - 1)
            with dve.Fori(0, blocks_of(dve)) as i:
                turn_did = Count("dve", found, ("moe",))

                def rest_of_tile(t):
                    dve.wait_ge(s_hi, i * MOE_TILES + (t + 1))
                    nc.vector.tensor_tensor(w_lo[:, t % SPLITS, :], ring[:, t % RING, :],
                                            w_hi[:, t % SPLITS, :].bitcast(F32), ALU.subtract).then_inc(s_used, 1)

                for t in range(KD):
                    rest_of_tile(t)
                for m in range(KD):
                    dve.wait_ge(moe_pe_done, in_turn(i, "back", m | 1))
                    nc.vector.scalar_tensor_tensor(out=hT[:, m, :], in0=banks[BACK_BANK[m]][:], scalar=modv[:,
                        5 * KD + m, 0:1], in1=hT[:, m, :], op0=ALU.mult, op1=ALU.add).then_inc(moe_dve_done,
                        turn_did.up(("acc", m)))
                    if m == 3:
                        rest_of_tile(KD)
                        rest_of_tile(KD + 1)
                for t in range(KD + 2, 2 * KD + SPLITS - 1):
                    rest_of_tile(t)
                dve.wait_ge(moe_pe_done, in_turn(i, "h"))
                dve.wait_ge(s_bias, i * 32 + 32)
                for n in range(4):
                    c = slice(n * 512, (n + 1) * 512)
                    nc.vector.tensor_tensor(hb[:, c], banks[n][:], e_bias[:, c], ALU.add).then_inc(moe_dve_done,
                        turn_did.up())
                dve.wait_ge(moe_dve_done, own_turn(i, turn_did))
                pairs = hb.rearrange("p (n two) -> p n two", two=2)
                nc.vector.tensor_scalar(g_part, pairs[:, :, 0], SWIGLU_LIMIT, None, ALU.min).then_inc(moe_dve_done,
                    turn_did.up(("g_part",)))
                nc.vector.tensor_scalar(u_part, pairs[:, :, 1], SWIGLU_LIMIT, -SWIGLU_LIMIT, ALU.min,
                    ALU.max).then_inc(moe_dve_done, turn_did.up())
                dve.wait_ge(moe_dve_done, own_turn(i, turn_did))
                nc.vector.scalar_tensor_tensor(out=u_part, in0=u_part, scalar=1.0, in1=g_part, op0=ALU.add,
                    op1=ALU.mult).then_inc(moe_dve_done, turn_did.up())
                dve.wait_ge(moe_dve_done, own_turn(i, turn_did))
                dve.wait_ge(moe_act_done, in_turn(i, "sig"))
                nc.vector.tensor_tensor(u_part, u_part, sig, ALU.mult).then_inc(moe_dve_done, turn_did.up(("act",)))
                for half in range(2):
                    c = slice(4 * half, 4 * half + 4)
                    dve.wait_ge(moe_act_done, in_turn(i, "xg_hi", half))
                    nc.vector.tensor_tensor(xg_lo[:, c, :], by_slot(4 + half), xg_hi[:, c, :].bitcast(F32),
                        ALU.subtract).then_inc(moe_dve_done, turn_did.up(("xg_kept", half)))
                for half in range(2):
                    c = slice(4 * half, 4 * half + 4)
                    dve.wait_ge(moe_act_done, in_turn(i, "act_hi", half))
                    nc.vector.tensor_tensor(act_lo[:, c, :], by_slot(6 + half), act_hi[:, c, :].bitcast(F32),
                        ALU.subtract).then_inc(moe_dve_done, turn_did.up(("act_t_kept", half)))
                for t in range(2 * KD + SPLITS - 1, MOE_TILES):
                    rest_of_tile(t)
                dve.wait_ge(moe_pe_done, in_turn(i, "y"))
                for n in range(2):
                    c = slice(n * 512, (n + 1) * 512)
                    nc.vector.tensor_tensor(y_slot[:, c], banks[4 + n][:], e_bias[:,
                        2 * D + n * 512:2 * D + (n + 1) * 512], ALU.add).then_inc(moe_dve_done,
                        turn_did.up(("y_kept", n)))
                dve.wait_ge(moe_dve_done, own_turn(i, turn_did))
                turn_did.close()
            nc.vector.memset(above[:, 0:1], 0.0).then_inc(dve_done, did.up(("last_y_kept",)))
            for m in range(KD):
                dve.wait_ge(pe_done, when("last_back", m))
                nc.vector.scalar_tensor_tensor(out=hT[:, m, :], in0=banks[BACK_BANK[m]][:], scalar=modv[:,
                    5 * KD + m, 0:1], in1=hT[:, m, :], op0=ALU.mult, op1=ALU.add).then_inc(dve_done,
                    did.up(("last_acc", m)))
            dve.wait_ge(dve_done, did.n)
            nc.vector.memset(above[:, 0:1], 0.0).then_inc(dve_done, did.up(("experts_done",)))
            rms_scaled(("final",), xT, hT, lambda k: col2("final_w", k))


SCAN = [(0, "c", 0), (1, "c", 1), (0, "c", 1), (1, "c", 0)]
for _b in range(TB):
    SCAN += [(0, "x", _b), (1, "x", TB - 1 - _b)]
SCAN_PREV = {s: s - 2 for s in range(2, len(SCAN))}
SCAN_BEFORE_X = {s: s - 1 if s > 2 * CB else None for s in range(2 * CB, len(SCAN))}


def _parts():
    out, left = [], TWO_PI
    for bits in (10, 11, 24):
        e = np.floor(np.log2(left))
        unit = 2.0 ** (e + 1 - bits)
        part = np.floor(left / unit) * unit if bits < 24 else float(np.float32(left))
        out.append(float(part))
        left -= part
    return out


TWO_PI_PARTS = _parts()
PI_BELOW = 3.1415925
BOUND = 1e30


def _cols(a):
    return np.ascontiguousarray(a.reshape(-1, P).T)


def _taps(w):
    k, c = w.shape
    return w.reshape(k, c // P, P).transpose(2, 1, 0).reshape(P, -1)


def _tiles(w):
    k, m = w.shape[0] // P, w.shape[1] // P
    full = -(-k // 8) * 8
    out = np.zeros((m, full // 8, P, 8, P), w.dtype)
    v = w.reshape(k, P, m, P).transpose(2, 0, 1, 3)
    for i in range(k):
        out[:, i // 8, :, i % 8, :] = v[:, i]
    return out.reshape(m * (full // 8), P, TILE)


def layer_tiles(inp, l):
    w = inp["w_in"][l]
    zeros = lambda n: np.zeros((D, n), w.dtype)
    cut, at = {}, 0
    for name, n in (("b", 256), ("c", 256), ("h", 256), ("q", 128), ("k", 128), ("gv", 256), ("gg", 256), ("ga", 32),
                    ("cq", 256), ("ckv", 128), ("kr", 32), ("a", 256), ("gate", 256)):
        cut[name] = w[:, at:at + n]
        at += n
    kr = cut["kr"]
    cut["misc"] = np.concatenate([cut["ga"], zeros(32), kr, kr[:, 16:], kr[:, :16]], 1)
    pick = lambda n: cut[n] if n in cut else cut[n[:-1]][:, int(n[-1]) * P:(int(n[-1]) + 1) * P]
    out = [_tiles(pick(n)) for n in PROJ[:10]]
    gv = cut["gv"].reshape(2, 4, P, MIX).transpose(0, 2, 1, 3).reshape(2, P, TILE)
    out.append(gv)
    out += [_tiles(pick(n)) for n in PROJ[10:]]
    uq = inp["w_mla_uq"][l].reshape(2, P, HEADS, NOPE + ROPE)
    uq = np.concatenate([uq, uq[..., 80:96], uq[..., 64:80]], 3).transpose(1, 0, 2, 3).reshape(1, P, TILE)
    ukv = inp["w_mla_ukv"][l].reshape(P, HEADS, 2, 64).transpose(0, 2, 1, 3).reshape(P, 512)
    up = np.zeros((P, 512), w.dtype)
    up[0:16, 0:128] = inp["w_gla_a_up"][l, 0]
    up[16:32, 128:256] = inp["w_gla_a_up"][l, 1]
    out += [uq, np.concatenate([ukv, up], 1)[None], _tiles(inp["w_out"][l])]
    ff = _tiles(inp["w_ffn_up"][l])
    out.append(np.stack([ff[:KF], ff[KF:]], 1).reshape(2 * KF, P, TILE))
    out.append(_tiles(inp["w_ffn_down"][l]))
    return out


def constants():
    f = np.float32
    t = np.arange(P)
    out = {"ident": np.eye(P), "ones": np.ones((P, P)), "ones_d": np.full((P, P), 1 / D),
           "ones_mix": np.full((P, P), 1 / MIX),
           "heads64": (t[:, None] // 64 == t[None] // 64) / 64, "upto": t[:, None] <= t[None],
           "after": t[:, None] > t[None], "eps2": np.full((P, 1), EPS2), "before": t[:, None] < t[None],
           "from": t[:, None] >= t[None], "eps": np.full((P, 1), EPS)}
    inv = f(10000.0) ** (-np.arange(0, ROPE, 2, dtype=f) / f(ROPE))
    out["inv_freq"] = inv[t % 16][:, None]
    out["sin_sign"] = np.where(t % 32 < 16, -1.0, 1.0)[:, None]
    share = []
    for w in POOL_WINDOWS:
        s = np.arange(GRID_W)
        share.append(f(1) / (np.clip(s + w - w // 2, 0, GRID_W) - np.clip(s - w // 2, 0, GRID_W)).astype(f))
    out["pool_share"] = np.tile(np.concatenate(share), (P, 1))
    return np.concatenate([out[n].astype(f) for n, _ in CONST_COLS], 1)


def block2_tiles(inp):
    w = inp["w_in_2"][0]
    xbc, dtw, z, pool = w[:, :2560], w[:, 2560:2608], w[:, 2608:4144], w[:, 4144:]
    dtw = np.concatenate([dtw, np.zeros((D, P - DT_W), w.dtype)], 1)
    z = z.reshape(4, 2, P, 3, 512).transpose(3, 0, 2, 1, 4).reshape(12, P, TILE)
    pw = np.concatenate([inp["pool_w_2"][0].transpose(1, 0, 2).reshape(P, 512), np.zeros((P, 512), w.dtype)], 1)
    router = np.concatenate([inp["router_w_2"][0], np.zeros((D, P - EXPERTS), w.dtype)], 1)
    return [_tiles(inp["w_mod_2"][0]), _tiles(dtw), _tiles(xbc), z, _tiles(pool), pw[None], _tiles(inp["w_out_2"][0]), _tiles(router)]


def layout(inputs):
    inp = {k: np.asarray(v) for k, v in inputs.items()}
    cols = [_cols(inp["ln_in_g"]), _cols(inp["ln_in_b"])]
    for l in range(DEPTH):
        cols += [_taps(inp["w_sc_conv"][l]), _cols(inp["b_gla_a"][l]), _cols(inp["g_gla_head"][l]),
                 _cols(inp["g_mla_q"][l]), _cols(inp["g_mla_kv"][l]), _taps(inp["w_cfm_dw"][l]),
                 _cols(inp["g_cfm_ln"][l]), _cols(inp["b_cfm_ln"][l]), _cols(inp["g_branch"][l]),
                 _cols(inp["ln1_g"][l]), _cols(inp["ln1_b"][l]), _taps(inp["w_ffn_dw"][l]),
                 _cols(inp["ln2_g"][l]), _cols(inp["ln2_b"][l])]
    cond = np.stack([inp["c_2"][0], inp["c_ctx_2"]], 1).reshape(KD, P, 2).transpose(1, 0, 2).reshape(P, 16)
    cols += [cond, _cols(inp["b_mod_2"]), _cols(inp["norm1_w_2"]), _cols(inp["norm2_w_2"]), _cols(inp["final_norm_w_2"]),
             _taps(inp["conv_w_2"][0]), _cols(inp["conv_b_2"]), _cols(inp["ssd_norm_w_2"]), _cols(inp["pool_scale_2"])]
    rows = [inp["dt_bias_2"], inp["a_log_2"], inp["d_skip_2"], inp["router_b_2"]]
    tiles = sum((layer_tiles(inp, l) for l in range(DEPTH)), []) + block2_tiles(inp)
    n = sum(len(t) for t in tiles)
    tiles.append(np.zeros((-n % RING, P, TILE), np.float32))
    return {"x": np.ascontiguousarray(inp["x"][0].T.reshape(KD, P, T).transpose(1, 0, 2).reshape(P, KD * T)),
            "positions": inp["positions"], "cols": np.concatenate(cols, 1), "consts": constants(),
            "wstream": np.concatenate(tiles, 0), "iota": np.tile(np.arange(T, dtype=np.float32), (P, 1)),
            "w1": inp["w1_2"].reshape(EXPERTS * KD, P, 2 * D), "w2": inp["w2_2"].reshape(EXPERTS * KD, P, D),
            "b1": inp["b1_2"].reshape(EXPERTS, 2 * D), "b2": inp["b2_2"].reshape(EXPERTS, D),
            "rows": np.concatenate([r.reshape(1, -1) for r in rows], 1),
            "ctx": np.ascontiguousarray(inp["ctx_2"][0].T.reshape(KD, P, CTX).transpose(1, 0, 2).reshape(P, KD * CTX))}


def kernel(**inputs):
    import concourse.bacc as _bacc
    from concourse.bass_utils import run_bass_kernel_spmd as _run

    arrays = layout(inputs)

    def program(marks):
        nc = _bacc.Bacc("TRN2", target_bir_lowering=False, num_devices=1)
        io = {n: nc.dram_tensor(f"in_{n}", a.shape, mybir.dt.from_np(a.dtype), kind="ExternalInput").ap()
              for n, a in arrays.items()}
        io["out"] = nc.dram_tensor("out_h", (P, KD * T), F32, kind="ExternalOutput").ap()
        found = {}
        build(nc, io, marks, found)
        return nc, found

    nc, _ = program(program(None)[1])
    r = _run(nc, [{f"in_{n}": a for n, a in arrays.items()}], core_ids=[0])
    out = r.results[0]["out_h"]
    return np.ascontiguousarray(out.reshape(P, KD, T).transpose(2, 1, 0).reshape(1, T, D))
```
